# Optimizing a Trainium2 kernel written in Bass

```python
import math
import jax, jax.numpy as jnp
from jax import lax
import numpy as np

D_MODEL = 1024
BATCH = 1
SEQ = 1024
DEPTH = 1

PLE_DIM = 256
N_HEADS = 4
QK_NOPE_DIM = 128
QK_ROPE_DIM = 64
V_HEAD_DIM = 128
Q_LORA_RANK = 256
KV_LORA_RANK = 128
ROPE_THETA = 10000.0
ATTN_WIDTH = N_HEADS * V_HEAD_DIM
Q_BLOCK = 128
CONV_GROUPS = 4
CONV_WIDTH = 512
CONV_K = 3
MIX_WIDTH = ATTN_WIDTH + CONV_WIDTH
IN_PROJ_WIDTH = Q_LORA_RANK + KV_LORA_RANK + QK_ROPE_DIM + 3 * CONV_WIDTH
N_EXPERTS = 32
TOP_K = 4
D_EXPERT = 1024
SWIGLU_ALPHA = 1.702
SWIGLU_LIMIT = 7.0
EXPERT_BLOCK = 128
EPS = 1e-6

kernel_name = "hymba_mla_shortconv_moe_ple"

def rmsnorm(x, g):
    xf = x.astype(jnp.float32)
    y = xf * lax.rsqrt(jnp.mean(xf * xf, axis=-1, keepdims=True) + EPS)
    return (y * g.astype(jnp.float32)).astype(x.dtype)

def apply_rope(x, positions):
    half = QK_ROPE_DIM // 2
    inv_freq = ROPE_THETA ** (-jnp.arange(half, dtype=jnp.float32) / half)
    ang = positions.astype(jnp.float32)[..., None] * inv_freq
    cos = jnp.cos(ang)[:, :, None, :]
    sin = jnp.sin(ang)[:, :, None, :]
    xf = x.astype(jnp.float32)
    x1, x2 = xf[..., :half], xf[..., half:]
    return jnp.concatenate([x1 * cos - x2 * sin, x1 * sin + x2 * cos], axis=-1).astype(x.dtype)

def mla(c_q, c_kv, k_pe, positions, q_norm, w_uq, kv_norm, w_ukv):
    B, S, _ = c_q.shape
    q = (rmsnorm(c_q, q_norm) @ w_uq).reshape(B, S, N_HEADS, QK_NOPE_DIM + QK_ROPE_DIM)
    q_nope, q_pe = q[..., :QK_NOPE_DIM], q[..., QK_NOPE_DIM:]
    q_pe = apply_rope(q_pe, positions)
    kv = (rmsnorm(c_kv, kv_norm) @ w_ukv).reshape(B, S, N_HEADS, QK_NOPE_DIM + V_HEAD_DIM)
    k_nope, v = kv[..., :QK_NOPE_DIM], kv[..., QK_NOPE_DIM:]
    k_pe = apply_rope(k_pe[:, :, None, :], positions)[:, :, 0, :]
    scale = (QK_NOPE_DIM + QK_ROPE_DIM) ** -0.5
    nqb = S // Q_BLOCK
    q_nope_b = q_nope.reshape(B, nqb, Q_BLOCK, N_HEADS, QK_NOPE_DIM).transpose(1, 0, 2, 3, 4)
    q_pe_b = q_pe.reshape(B, nqb, Q_BLOCK, N_HEADS, QK_ROPE_DIM).transpose(1, 0, 2, 3, 4)
    k_pos = jnp.arange(S)

    def q_block(args):
        qn, qp, i = args
        s = (jnp.einsum('bqhd,bkhd->bhqk', qn, k_nope)
             + jnp.einsum('bqhr,bkr->bhqk', qp, k_pe)).astype(jnp.float32) * scale
        q_pos = i * Q_BLOCK + jnp.arange(Q_BLOCK)
        causal = k_pos[None, :] <= q_pos[:, None]
        s = jnp.where(causal, s, -jnp.inf)
        prob = jax.nn.softmax(s, axis=-1).astype(v.dtype)
        return jnp.einsum('bhqk,bkhd->bqhd', prob, v)

    out = lax.map(q_block, (q_nope_b, q_pe_b, jnp.arange(nqb)))
    return out.transpose(1, 0, 2, 3, 4).reshape(B, S, ATTN_WIDTH)

def short_conv(b_gate, c_gate, val, conv_w):
    S = val.shape[1]
    u = c_gate * val
    u_pad = jnp.pad(u, ((0, 0), (CONV_K - 1, 0), (0, 0)))
    y = conv_w[0] * u_pad[:, 0:S]
    for k in range(1, CONV_K):
        y = y + conv_w[k] * u_pad[:, k:k + S]
    return b_gate * y

def clamped_swiglu(h):
    gate, up = h[..., :D_EXPERT], h[..., D_EXPERT:]
    gate = jnp.minimum(gate, SWIGLU_LIMIT)
    up = jnp.clip(up, -SWIGLU_LIMIT, SWIGLU_LIMIT)
    return gate * jax.nn.sigmoid(SWIGLU_ALPHA * gate) * (up + 1)

def moe(x, w_router, b_router, w1, b1, w2, b2):
    B, S, D = x.shape
    N = B * S
    xt = x.reshape(N, D)
    logits = (xt @ w_router + b_router).astype(jnp.float32)
    top_v, top_i = lax.top_k(logits, TOP_K)
    gates = jax.nn.softmax(top_v, axis=-1)
    M = N * TOP_K
    e = top_i.reshape(M)
    tok = jnp.repeat(jnp.arange(N, dtype=jnp.int32), TOP_K)
    g = gates.reshape(M)
    order = jnp.argsort(e)
    e_s, tok_s, g_s = e[order], tok[order], g[order]
    counts = jnp.bincount(e, length=N_EXPERTS)
    starts = jnp.cumsum(counts) - counts
    padded = ((counts + EXPERT_BLOCK - 1) // EXPERT_BLOCK) * EXPERT_BLOCK
    pad_ends = jnp.cumsum(padded)
    pad_starts = pad_ends - padded
    dest = pad_starts[e_s] + jnp.arange(M) - starts[e_s]
    n_blocks = -(-M // EXPERT_BLOCK) + N_EXPERTS
    P = n_blocks * EXPERT_BLOCK
    row_tok = jnp.full((P,), N, dtype=jnp.int32).at[dest].set(tok_s)
    row_gate = jnp.zeros((P,), dtype=jnp.float32).at[dest].set(g_s)
    blk_expert = jnp.clip(jnp.searchsorted(pad_ends, jnp.arange(n_blocks) * EXPERT_BLOCK, side='right'),
                          0, N_EXPERTS - 1)
    x_pad = jnp.concatenate([xt, jnp.zeros((1, D), xt.dtype)], axis=0)

    def expert_block(args):
        rows, eid = args
        xb = x_pad[rows]
        hb = clamped_swiglu(xb @ w1[eid] + b1[eid])
        return hb @ w2[eid] + b2[eid]

    y = lax.map(expert_block, (row_tok.reshape(n_blocks, EXPERT_BLOCK), blk_expert))
    y = y.reshape(P, D) * row_gate[:, None].astype(y.dtype)
    out = jax.ops.segment_sum(y, row_tok, num_segments=N + 1)[:N]
    return out.reshape(B, S, D)

def setup_inputs(seed: int = 0) -> dict:
    key = jax.random.key(seed)
    ks = jax.random.split(key, 32)
    f32 = jnp.float32

    def nrm(k, shape, fan_in):
        return jax.random.normal(k, shape, f32) * (fan_in ** -0.5)

    def gain(k, shape):
        return 1.0 + 0.01 * jax.random.normal(k, shape, f32)

    L = DEPTH
    return {
        "x": jax.random.normal(ks[0], (BATCH, SEQ, D_MODEL), f32),
        "p": jax.random.normal(ks[1], (DEPTH, BATCH, SEQ, PLE_DIM), f32),
        "positions": jnp.broadcast_to(jnp.arange(SEQ, dtype=jnp.int32), (BATCH, SEQ)),
        "mix_norm": gain(ks[2], (L, D_MODEL)),
        "w_in": nrm(ks[3], (L, D_MODEL, IN_PROJ_WIDTH), D_MODEL),
        "q_norm": gain(ks[4], (L, Q_LORA_RANK)),
        "w_uq": nrm(ks[5], (L, Q_LORA_RANK, N_HEADS * (QK_NOPE_DIM + QK_ROPE_DIM)), Q_LORA_RANK),
        "kv_norm": gain(ks[6], (L, KV_LORA_RANK)),
        "w_ukv": nrm(ks[7], (L, KV_LORA_RANK, N_HEADS * (QK_NOPE_DIM + V_HEAD_DIM)), KV_LORA_RANK),
        "conv_w": nrm(ks[8], (L, CONV_K, CONV_WIDTH), CONV_K),
        "attn_out_norm": gain(ks[9], (L, ATTN_WIDTH)),
        "conv_out_norm": gain(ks[10], (L, CONV_WIDTH)),
        "w_o": nrm(ks[11], (L, MIX_WIDTH, D_MODEL), MIX_WIDTH),
        "moe_norm": gain(ks[12], (L, D_MODEL)),
        "w_router": nrm(ks[13], (L, D_MODEL, N_EXPERTS), D_MODEL),
        "b_router": 0.01 * jax.random.normal(ks[14], (L, N_EXPERTS), f32),
        "w1": nrm(ks[15], (L, N_EXPERTS, D_MODEL, 2 * D_EXPERT), D_MODEL),
        "b1": 0.01 * jax.random.normal(ks[16], (L, N_EXPERTS, 2 * D_EXPERT), f32),
        "w2": nrm(ks[17], (L, N_EXPERTS, D_EXPERT, D_MODEL), D_EXPERT),
        "b2": 0.01 * jax.random.normal(ks[18], (L, N_EXPERTS, D_MODEL), f32),
        "ple_norm": gain(ks[19], (L, D_MODEL)),
        "w_ple_gate": nrm(ks[20], (L, D_MODEL, D_MODEL), D_MODEL),
        "w_ple_proj": nrm(ks[21], (L, PLE_DIM, D_MODEL), PLE_DIM),
        "ple_post_norm": gain(ks[22], (L, D_MODEL)),
        "final_norm": gain(ks[23], (D_MODEL,)),
    }

def reference(x, p, positions, mix_norm, w_in, q_norm, w_uq, kv_norm, w_ukv, conv_w,
              attn_out_norm, conv_out_norm, w_o, moe_norm, w_router, b_router, w1, b1, w2, b2,
              ple_norm, w_ple_gate, w_ple_proj, ple_post_norm, final_norm):
    split_pts = list(np.cumsum([Q_LORA_RANK, KV_LORA_RANK, QK_ROPE_DIM, CONV_WIDTH, CONV_WIDTH]))
    h = x
    for i in range(DEPTH):
        z = rmsnorm(h, mix_norm[i]) @ w_in[i]
        c_q, c_kv, k_pe, b_gate, c_gate, val = jnp.split(z, split_pts, axis=-1)
        attn = mla(c_q, c_kv, k_pe, positions, q_norm[i], w_uq[i], kv_norm[i], w_ukv[i])
        conv = short_conv(b_gate, c_gate, val, conv_w[i])
        mixed = jnp.concatenate([rmsnorm(attn, attn_out_norm[i]),
                                 rmsnorm(conv, conv_out_norm[i])], axis=-1)
        h = h + mixed @ w_o[i]
        h = h + moe(rmsnorm(h, moe_norm[i]), w_router[i], b_router[i], w1[i], b1[i], w2[i], b2[i])
        gate = jax.nn.sigmoid(rmsnorm(h, ple_norm[i]) @ w_ple_gate[i])
        ple = rmsnorm(p[i] @ w_ple_proj[i], ple_post_norm[i])
        h = h + gate * ple
    return rmsnorm(h, final_norm)


_drawn_inputs = setup_inputs


def setup_inputs(seed=0):
    import zlib

    import numpy as np

    out = dict(_drawn_inputs(seed))
    spreads = {}
    factors = {'q_norm': 10.173,
     'attn_out_norm': 15.415,
     'conv_out_norm': 13.957,
     'b1': 27.718,
     'b2': 31.799,
     'ple_norm': 49.025,
     'ple_post_norm': 52.854,
     'final_norm': 33.83,
     'kv_norm': 2.885,
     'moe_norm': 5.047,
     'b_router': 5.328}
    for name, (base, spread) in spreads.items():
        noise = np.random.default_rng([zlib.crc32(name.encode()), seed]).standard_normal(out[name].shape)
        drawn = base * np.exp(spread * noise) if base else spread * noise
        out[name] = __import__('jax').numpy.asarray(drawn.astype(out[name].dtype))
    for name, factor in factors.items():
        out[name] = (out[name] * factor).astype(out[name].dtype)
    return out
```

```python
import math
from contextlib import ExitStack, contextmanager

import concourse.bass as bass
from concourse import mybir

F32 = mybir.dt.float32
F32R = mybir.dt.float32r
BF16 = mybir.dt.bfloat16
I32 = mybir.dt.int32
U32 = mybir.dt.uint32
ALU = mybir.AluOpType
ACT = mybir.ActivationFunctionType
AX = mybir.AxisListType

P = 128
BANK = 512
EPS = 1e-6
ROPE_THETA = 10000.0
N_HEADS, NOPE, ROPE, VDIM = 4, 128, 64, 128
Q_LORA, KV_LORA = 256, 128
TOP_K = 4
ALPHA, LIMIT = 1.702, 7.0
MASKED = -1e30


class Chain:

    def __init__(self, eng, sem):
        self.eng, self.sem, self.n = eng, sem, 0

    def done(self, ins):
        ins.then_inc(self.sem, 1)
        self.n = self.n + 1
        self.eng.wait_ge(self.sem, self.n)


RAW, HL = 6, 3
HALF_K = 4


def blocks_bound(tokens, experts):
    return tokens * TOP_K // P + experts


@contextmanager
def phase_block(nc, sems):
    with nc.Block() as block:
        yield block
    nc.all_engine_barrier()
    nc.clear_and_free_semaphores(sems)
    nc.all_engine_barrier()


def split_mm(pe, out, a_hi, a_lo, b_hi, b_lo, first, last):
    pe.matmul(out, a_hi, b_hi, start=first, stop=False)
    pe.matmul(out, a_lo, b_hi, start=False, stop=False)
    return pe.matmul(out, a_hi, b_lo, start=False, stop=last)


def mix_phase(nc, dram, keep):
    x, w_in = dram["x"], dram["w_in"]
    S, D = x.shape[1], x.shape[2]
    T = S // P
    KD = D // P
    HALF = S // BANK
    CW = dram["conv_w"].shape[2]
    CI = CW // P
    NBLK = blocks_bound(S, dram["w1"].shape[1])
    ATT0 = Q_LORA + KV_LORA + ROPE
    GATE_B, GATE_C, VALUE = ATT0, ATT0 + CW, ATT0 + 2 * CW
    SCALE = float(NOPE + ROPE) ** -0.5
    TWO_PI = 2 * math.pi
    PI_A = 6.28125
    PI_B = 0.0019350051879882812
    PI_C = TWO_PI - PI_A - PI_B
    MAGIC = 12582912.0

    xh = keep["wide"][:, 0, :].rearrange("p (k s) -> p k s", k=KD)
    xl = keep["wide"][:, 1, :].rearrange("p (k s) -> p k s", k=KD)
    conv_hi, conv_lo = keep["conv"][:, 0], keep["conv"][:, 1]
    att_hi = keep["wide"][:, 0, 0:4 * S].rearrange("p (h s) -> p h s", h=N_HEADS)
    att_lo = keep["wide"][:, 1, 0:4 * S].rearrange("p (h s) -> p h s", h=N_HEADS)

    with ExitStack() as ctx:
        def sb(name, shape, dt=F32):
            return ctx.enter_context(nc.sbuf_tensor(name, shape, dt))

        sems = []

        def sem(name):
            sems.append(nc.alloc_semaphore(name=name))
            return sems[-1]

        ws = sb("ws", [P, 3, 2, S], F32R)
        ws_k = ws[:].rearrange("p r z (k m) -> p r z k m", k=KD)
        ar = sb("mix_arena", [P, 21 * 1024])
        x_all = ar[:, 0:8 * D].rearrange("p (t d) -> p t d", t=T)
        tmp = [ar[:, i * S:(i + 1) * S] for i in range(3)]
        cqn = ar[:, 0:2 * S].rearrange("p (k s) -> p k s", k=2)
        ckvn = ar[:, 2 * S:3 * S]
        gate_c = ar[:, 3 * S:4 * S]
        u = ar[:, 4 * S:4 * S + S + 2]
        y = ar[:, 4 * S + 1536:5 * S + 1536]
        keys = ar[:, 3 * S:7 * S].rearrange("p (h s) -> p h s", h=N_HEADS)
        sq_kv = ar[:, 7 * S:8 * S]
        xn = ar[:, 8 * S:10 * S].rearrange("p (b d) -> p b d", b=2)
        sq_conv = ar[:, 8 * S:12 * S].rearrange("p (i s) -> p i s", i=CI)
        prob = ar[:, 8 * S:10 * S].rearrange("p (b s) -> p b s", b=2)
        values = ar[:, 10 * S:14 * S].rearrange("p (t c) -> p t c", t=T)
        q_nope = ar[:, 7 * S:8 * S]
        q_pe = ar[0:ROPE, 2 * S:3 * S]
        pt = [ar[:, 18 * S:19 * S], ar[:, 15 * S:16 * S]]
        junk_o = ar[:, 14 * S + 512:14 * S + 512 + P]
        g_mix = ar[:, 12 * S:13 * S]
        sq_cq = ar[:, 12 * S:14 * S].rearrange("p (k s) -> p k s", k=2)
        junk = ar[:, 13 * S:14 * S]
        raw = ar[:, 14 * S:17 * S].rearrange("p (r k m) -> p r k m", r=3, k=KD)
        w_qh = ar[:, 14 * S:14 * S + 512].rearrange("p (k m) -> p k m", k=2)
        w_ukv = ar[:, 15 * S:16 * S]
        r_q, r_kv = ar[:, 17 * S:18 * S], ar[:, 18 * S:19 * S]
        rope_t = r_q[0:ROPE]
        cossin = ar[:, 19 * S:20 * S]
        k_pe = ar[0:ROPE, 20 * S:21 * S]
        mask = sb("mask", [P, P])
        o_sb = sb("o_sb", [P, 2, P])
        angle_c = sb("angle_c", [P, 4])
        ss = sb("ss", [P, 3, T])
        g_q = sb("g_q", [P, 2])
        g_kv = sb("g_kv", [P, 1])
        g_att = sb("g_att", [P, N_HEADS])
        g_conv = sb("g_conv", [P, CI])
        taps = sb("taps", [P, 3, CI])
        negm = sb("negm", [P, 4])
        psum_p = sb("psum_p", [P, 8])
        ss_att = keep["ss_att"]

        psum = ctx.enter_context(nc.psum_tensor("mix_psum", [P, 8, BANK], F32))

        x_loaded = [sem(f"x_loaded{t}") for t in range(T)]
        par_loaded = sem("par_loaded")
        g_loaded = sem("g_loaded")
        pos_loaded = sem("pos_loaded")
        ws_loaded = [sem(f"ws_loaded{r}") for r in range(3)]
        ukv_loaded = sem("ukv_loaded")
        wqh_loaded = sem("wqh_loaded")
        consts_made = sem("consts_made")
        zero_made = sem("zero_made")
        zero_stored = sem("zero_stored")
        x_stats = sem("x_stats")
        xn_made = sem("xn_made")
        x_turned = sem("x_turned")
        xt_hi_made = sem("xt_hi_made")
        xt_lo_made = sem("xt_lo_made")
        ws_hi_made = sem("ws_hi_made")
        ws_lo_made = sem("ws_lo_made")
        tile_done = sem("tile_done")
        c_copied = sem("c_copied")
        u_made = sem("u_made")
        y_made = sem("y_made")
        y_squared = sem("y_squared")
        conv_hi_made = sem("conv_hi_made")
        conv_lo_made = sem("conv_lo_made")
        lat_squared = sem("lat_squared")
        lat_copied = sem("lat_copied")
        kpe_made = sem("kpe_made")
        conv_ss_done = sem("conv_ss_done")
        lat_ss_done = sem("lat_ss_done")
        lat_std = sem("lat_std")
        lat_normed = sem("lat_normed")
        k_done = sem("k_done")
        k_copied = sem("k_copied")
        v_done = sem("v_done")
        v_copied = sem("v_copied")
        q_done = sem("q_done")
        qn_copied = sem("qn_copied")
        qpe_made = sem("qpe_made")
        scores_done = sem("scores_done")
        negmax_made = sem("negmax_made")
        prob_made = sem("prob_made")
        prob_turned = sem("prob_turned")
        pt_made = sem("pt_made")
        o_done = sem("o_done")
        o_scaled = sem("o_scaled")
        o_turned = sem("o_turned")
        ot_hi_made = sem("ot_hi_made")
        ot_lo_made = sem("ot_lo_made")
        o_squared = sem("o_squared")
        angles_made = sem("angles_made")
        sines_made = sem("sines_made")
        conv_ss_copied = sem("conv_ss_copied")
        act_passed = sem("act_passed")
        dve_passed = sem("dve_passed")
        pe_passed = sem("pe_passed")
        sp_passed = sem("sp_passed")
        act_step = sem("act_step")
        dve_step = sem("dve_step")

        s_bank = [psum[:, 2 * b:2 * b + 2, :].rearrange("p b n -> p (b n)") for b in range(4)]
        turn_ps = s_bank[2]
        w_in3 = w_in[0].rearrange("(k p) n -> p k n", p=P)
        w_uq3 = dram["w_uq"][0].rearrange("(k p) n -> p k n", p=P)
        QH = NOPE + ROPE
        x_rows = x[0].rearrange("(t p) d -> p t d", p=P)

        block = ctx.enter_context(phase_block(nc, sems))

        @block.sync
        def _(sp):
            for t in range(T):
                sp.dma_start(x_all[:, t], x_rows[:, t]).then_inc(x_loaded[t], 16)
                if t == 0:
                    sp.dma_start(g_mix, dram["mix_norm"][0:1, :].partition_broadcast(P)).then_inc(g_loaded, 16)
            for r, col in enumerate([GATE_C, VALUE, GATE_B]):
                sp.dma_start(raw[:, r], w_in3[:, :, col:col + P]).then_inc(ws_loaded[r], 16)
            with sp.Fori(1, CI) as i:
                for r, col in enumerate([GATE_C, VALUE, GATE_B]):
                    sp.wait_ge(ws_lo_made, 3 * i + r - 2)
                    sp.dma_start(raw[:, r], w_in3[:, :, bass.ds(i * P + col, P)]).then_inc(ws_loaded[r], 16)
            for r in range(3):
                sp.wait_ge(ws_lo_made, 3 * CI + r - 2)
                sp.dma_start(raw[:, r], w_in3[:, :, r * P:(r + 1) * P]).then_inc(ws_loaded[r], 16)
            c0, hr = Q_LORA + KV_LORA, ROPE // 2
            sp.wait_ge(ws_lo_made, 3 * CI + 1)
            sp.dma_start(raw[:, 0, :, 0:ROPE], w_in3[:, :, c0:c0 + ROPE]).then_inc(ws_loaded[0], 16)
            sp.dma_start(raw[:, 0, :, ROPE:ROPE + hr], w_in3[:, :, c0 + hr:c0 + ROPE]).then_inc(ws_loaded[0], 16)
            sp.dma_start(raw[:, 0, :, ROPE + hr:P], w_in3[:, :, c0:c0 + hr]).then_inc(ws_loaded[0], 16)
            sp.wait_ge(ws_lo_made, 3 * CI + 2)
            sp.dma_start(w_ukv, dram["w_ukv"][0]).then_inc(ukv_loaded, 16)
            sp.wait_ge(ws_lo_made, 3 * CI + 4)
            with sp.Fori(0, N_HEADS) as h:
                with sp.If(h > 0):
                    sp.wait_ge(q_done, h * 4)
                    sp.sem_inc(sp_passed, 1)
                c0 = h * QH
                sp.dma_start(w_qh[:, :, 0:QH], w_uq3[:, :, bass.ds(c0, QH)]).then_inc(wqh_loaded, 16)
                sp.dma_start(w_qh[:, :, QH:QH + hr], w_uq3[:, :, bass.ds(c0 + NOPE + hr, hr)]).then_inc(wqh_loaded, 16)
                sp.dma_start(w_qh[:, :, QH + hr:QH + ROPE], w_uq3[:, :, bass.ds(c0 + NOPE, hr)]).then_inc(wqh_loaded, 16)

        @block.gpsimd
        def _(pool):
            pool.memset(keep["ident"][:], 0.0).then_inc(consts_made, 1)
            pool.memset(mask[:], 0.0).then_inc(consts_made, 1)
            pool.memset(keep["ones"][:], 1.0).then_inc(consts_made, 1)
            pool.memset(keep["eps"][:], EPS).then_inc(consts_made, 1)
            pool.wait_ge(consts_made, 4)
            pool.affine_select(out=keep["ident"][:], in_=keep["ident"][:], compare_op=ALU.not_equal, fill=1.0,
                               base=0, pattern=[[-1, P]], channel_multiplier=1).then_inc(consts_made, 1)
            pool.affine_select(out=mask[:], in_=mask[:], compare_op=ALU.is_ge, fill=MASKED,
                               base=0, pattern=[[-1, P]], channel_multiplier=1).then_inc(consts_made, 1)
            with nc.allow_non_contiguous_dma(reason="small parameters, once"):
                pool.dma_start(angle_c[:], dram["angle_consts"]).then_inc(par_loaded, 16)
                pool.dma_start(g_q[:], dram["q_norm"][0].rearrange("(k p) -> p k", p=P)).then_inc(par_loaded, 16)
                pool.dma_start(g_kv[:], dram["kv_norm"][0].rearrange("(k p) -> p k", p=P)).then_inc(par_loaded, 16)
                pool.dma_start(g_att[:], dram["attn_out_norm"][0].rearrange("(k p) -> p k", p=P)).then_inc(par_loaded, 16)
                pool.dma_start(g_conv[:], dram["conv_out_norm"][0].rearrange("(k p) -> p k", p=P)).then_inc(par_loaded, 16)
                for j in range(3):
                    pool.dma_start(taps[:, j], dram["conv_w"][0, j].rearrange("(k p) -> p k", p=P)).then_inc(par_loaded, 16)
            pool.wait_ge(xn_made, T)
            pool.dma_start(tmp[2].bitcast(I32), dram["positions"][0:1, :].partition_broadcast(P)).then_inc(pos_loaded, 16)
            pool.wait_ge(pos_loaded, 16)
            pool.wait_ge(ws_lo_made, 3 * CI + 3)
            pool.memset(raw[:, 2], 0.0).then_inc(zero_made, 1)
            pool.wait_ge(zero_made, 1)
            y_rows = dram["y_slots"].rearrange("(b p) d -> b p d", p=P)
            zeros = raw[:, 2].rearrange("p k m -> p (k m)")
            for n in range(NBLK):
                pool.dma_start(y_rows[n], zeros).then_inc(zero_stored, 16)
            pool.wait_ge(zero_stored, NBLK * 16)

        PAR = 16 * 8
        CONSTS = 6

        @block.scalar
        def _(act):
            act.wait_ge(consts_made, CONSTS)
            for t in range(T):
                act.wait_ge(x_loaded[t], 16)
                act.activation(junk, x_all[:, t], ACT.Square, accum_out=ss[:, 0, t:t + 1]).then_inc(act_step, 1)
                act.wait_ge(act_step, t + 1)
            act.activation(ss[:, 1], ss[:, 0], ACT.Sqrt, scale=1.0 / D, bias=keep["eps"][:, 0:1]).then_inc(x_stats, 1)
            with act.Fori(0, T // 2) as pair:
                t0 = pair * 2
                for b in range(2):
                    for q in range(2):
                        act.wait_ge(x_turned, 2 * t0 + (2 * b + q + 1))
                        act.activation(xh[:, 4 * q:4 * q + 4, bass.ds((t0 + b) * P, P)],
                                       psum[:, 2 * b + q].rearrange("p (k m) -> p k m", k=4),
                                       ACT.Copy).then_inc(xt_hi_made, 1)

            def split_hi(r):
                act.activation(ws[:, r, 0], raw[:, r].rearrange("p k m -> p (k m)"), ACT.Copy).then_inc(ws_hi_made, 1)

            for r in range(3):
                act.wait_ge(ws_loaded[r], 16)
                split_hi(r)
            act.wait_ge(par_loaded, PAR)
            act.wait_ge(angles_made, 1)
            act.activation(cossin, tmp[1], ACT.Sin).then_inc(sines_made, 1)
            with act.Fori(0, CI) as i:
                with act.If(i > 0):
                    act.wait_ge(u_made, i)
                    act.sem_inc(act_passed, 1)
                act.wait_ge(tile_done, 3 * i + 1)
                act.activation(gate_c, s_bank[0], ACT.Copy).then_inc(c_copied, 1)
                for r in range(3):
                    act.wait_ge(tile_done, 3 * i + r + 1)
                    act.wait_ge(ws_loaded[r], i * 16 + 32)
                    split_hi(r)
                act.wait_ge(y_made, i + 1)
                act.activation(sq_conv[:, bass.ds(i, 1)], y.rearrange("p (o s) -> p o s", o=1), ACT.Square).then_inc(y_squared, 1)
                act.activation(conv_hi[:, bass.ds(i, 1)], y.rearrange("p (o s) -> p o s", o=1), ACT.Copy,
                               scale=g_conv[:, bass.ds(i, 1)]).then_inc(conv_hi_made, 1)
            act.wait_ge(tile_done, 3 * CI + 1)
            act.wait_ge(ws_loaded[0], 16 * (CI + 1) + 48)
            split_hi(0)
            for m, dst in enumerate([sq_cq[:, 0], sq_cq[:, 1], sq_kv]):
                act.wait_ge(tile_done, 3 * CI + m + 1)
                act.activation(dst, s_bank[m], ACT.Square).then_inc(lat_squared, 1)
            act.wait_ge(lat_ss_done, 1)
            act.activation(r_kv, s_bank[2], ACT.Sqrt, scale=1.0 / KV_LORA, bias=keep["eps"][:, 0:1]).then_inc(lat_std, 1)
            act.wait_ge(lat_ss_done, 2)
            act.wait_ge(kpe_made, 1)
            act.activation(r_q, s_bank[1], ACT.Sqrt, scale=1.0 / Q_LORA, bias=keep["eps"][:, 0:1]).then_inc(lat_std, 1)
            act.wait_ge(conv_ss_done, 1)
            act.activation(keep["ss_conv"][:], psum[:, 6, 0:T], ACT.Copy).then_inc(conv_ss_copied, 1)
            for h in range(N_HEADS):
                act.wait_ge(k_done, h + 1)
                act.activation(keys[:, h], s_bank[h % 2], ACT.Copy).then_inc(k_copied, 1)
            with act.Fori(0, T // 2) as pair:
                t0 = pair * 2
                for b in range(2):
                    act.wait_ge(v_done, t0 + b + 1)
                    act.activation(values[:, bass.ds(t0 + b, 1)], psum[:, 4 + b:5 + b], ACT.Copy).then_inc(v_copied, 1)
            with act.Fori(0, N_HEADS) as h:
                act.wait_ge(q_done, h * 4 + 4)
                act.activation(q_nope, s_bank[0], ACT.Copy).then_inc(qn_copied, 1)

                def exp(i):
                    b, n = i % 2, (i + 1) * P
                    act.wait_ge(negmax_made, h * T + i + 1)
                    if i >= 2:
                        act.wait_ge(prob_turned, h * T + i - 1)
                    act.activation(prob[:, b, 0:n], s_bank[b][:, 0:n], ACT.Exp, scale=SCALE, bias=negm[:, b:b + 1],
                                   accum_out=psum_p[:, i % 4:i % 4 + 1]).then_inc(prob_made, 1)

                def turned_o(i):
                    b = i % 2
                    act.wait_ge(o_turned, h * T + i + 1)
                    act.activation(att_hi[:, bass.ds(h, 1), i * P:(i + 1) * P], psum[:, 7:8, 0:P],
                                   ACT.Copy, scale=g_att[:, bass.ds(h, 1)]).then_inc(ot_hi_made, 1)

                def square_o(i):
                    if i == 0:
                        with act.If(h > 0):
                            act.wait_ge(o_squared, h * T)
                            act.sem_inc(act_passed, 1)
                    else:
                        act.wait_ge(o_squared, h * T + i)
                    act.wait_ge(o_scaled, h * T + i + 1)
                    act.activation(junk_o, o_sb[:, i % 2], ACT.Square,
                                   accum_out=ss_att[:, i, bass.ds(h, 1)]).then_inc(o_squared, 1)

                exp(0)
                for i in range(T):
                    b, n = i % 2, (i + 1) * P
                    if i + 1 < T:
                        exp(i + 1)
                    act.wait_ge(prob_turned, h * T + i + 1)
                    if i >= 2:
                        act.wait_ge(o_done, h * T + i - 1)
                    act.activation(pt[b][:, 0:n], turn_ps[:, 0:n], ACT.Copy).then_inc(pt_made, 1)
                    if i >= 1:
                        square_o(i - 1)
                    if i >= 2:
                        turned_o(i - 2)
                square_o(T - 1)
                turned_o(T - 2)
                turned_o(T - 1)

        @block.vector
        def _(dve):
            ch = Chain(dve, dve_step)
            dve.wait_ge(x_stats, 1)
            ch.done(dve.reciprocal(ss[:, 2], ss[:, 1]))
            dve.wait_ge(par_loaded, PAR)
            dve.wait_ge(g_loaded, 16)

            def turned_lo(t, b):
                for q in range(2):
                    dve.wait_ge(xt_hi_made, 2 * t + q + 1)
                    dve.tensor_tensor(xl[:, 4 * q:4 * q + 4, bass.ds(t * P, P)],
                                      psum[:, 2 * b + q].rearrange("p (k m) -> p k m", k=4),
                                      xh[:, 4 * q:4 * q + 4, bass.ds(t * P, P)].bitcast(F32),
                                      ALU.subtract).then_inc(xt_lo_made, 1)

            dve.scalar_tensor_tensor(out=xn[:, 0], in0=x_all[:, 0], scalar=ss[:, 2, 0:1], in1=g_mix,
                                     op0=ALU.mult, op1=ALU.mult).then_inc(xn_made, 1)
            dve.scalar_tensor_tensor(out=xn[:, 1], in0=x_all[:, 1], scalar=ss[:, 2, 1:2], in1=g_mix,
                                     op0=ALU.mult, op1=ALU.mult).then_inc(xn_made, 1)
            with dve.Fori(0, T // 2 - 1) as pair:
                for b in range(2):
                    t = pair * 2 + b
                    turned_lo(t, b)
                    dve.scalar_tensor_tensor(out=xn[:, b:b + 1], in0=x_all[:, bass.ds(t + 2, 1)],
                                             scalar=ss[:, 2, bass.ds(t + 2, 1)],
                                             in1=g_mix.rearrange("p (o d) -> p o d", o=1),
                                             op0=ALU.mult, op1=ALU.mult).then_inc(xn_made, 1)
            turned_lo(T - 2, 0)
            turned_lo(T - 1, 1)

            def split_lo(n, r):
                dve.wait_ge(ws_hi_made, n + 1)
                dve.tensor_tensor(ws[:, r, 1], raw[:, r].rearrange("p k m -> p (k m)"), ws[:, r, 0].bitcast(F32),
                                  ALU.subtract).then_inc(ws_lo_made, 1)

            for r in range(3):
                split_lo(r, r)
            dve.wait_ge(pos_loaded, 16)
            ch.done(dve.tensor_copy(tmp[0], tmp[2].bitcast(I32)))
            ch.done(dve.tensor_scalar(tmp[1], tmp[0], angle_c[:, 0:1], None, ALU.mult))
            ch.done(dve.tensor_scalar(tmp[0], tmp[1], 1.0 / TWO_PI, angle_c[:, 1:2], ALU.mult, ALU.add))
            ch.done(dve.tensor_scalar(tmp[2], tmp[0], MAGIC, MAGIC, ALU.add, ALU.subtract))
            for turn_part in (PI_A, PI_B, PI_C):
                ch.done(dve.scalar_tensor_tensor(out=tmp[1], in0=tmp[2], scalar=-turn_part, in1=tmp[1],
                                                 op0=ALU.mult, op1=ALU.add))
            ch.done(dve.tensor_scalar(tmp[1], tmp[1], angle_c[:, 2:3], 3.1415925, ALU.add, ALU.min))
            dve.tensor_scalar(tmp[1], tmp[1], -3.1415925, None, ALU.max).then_inc(angles_made, 1)
            ch.done(dve.memset(u[:, 0:2], 0.0))
            dve.wait_ge(sines_made, 1)
            ch.done(dve.tensor_scalar(cossin, cossin, angle_c[:, 3:4], None, ALU.mult))

            first = ch.n
            with dve.Fori(0, CI) as i:
                ch.n = i * 3 + first
                tap = [taps[:, j, bass.ds(i, 1)] for j in range(3)]
                split_lo(i * 3 + 3, 0)
                dve.wait_ge(c_copied, i + 1)
                dve.wait_ge(tile_done, i * 3 + 2)
                dve.tensor_tensor(u[:, 2:S + 2], s_bank[1], gate_c, ALU.mult).then_inc(u_made, 1)
                split_lo(i * 3 + 4, 1)
                with dve.If(i > 0):
                    dve.wait_ge(y_squared, i)
                    dve.wait_ge(conv_lo_made, i)
                    dve.sem_inc(dve_passed, 1)
                dve.wait_ge(u_made, i + 1)
                ch.done(dve.tensor_scalar(y, u[:, 0:S], tap[0], None, ALU.mult))
                ch.done(dve.scalar_tensor_tensor(out=y, in0=u[:, 1:S + 1], scalar=tap[1], in1=y, op0=ALU.mult, op1=ALU.add))
                ch.done(dve.scalar_tensor_tensor(out=y, in0=u[:, 2:S + 2], scalar=tap[2], in1=y, op0=ALU.mult, op1=ALU.add))
                split_lo(i * 3 + 5, 2)
                dve.wait_ge(tile_done, i * 3 + 3)
                dve.tensor_tensor(y, s_bank[2], y, ALU.mult).then_inc(y_made, 1)
                dve.wait_ge(y_made, i + 1)
                dve.wait_ge(conv_hi_made, i + 1)
                dve.scalar_tensor_tensor(out=conv_lo[:, bass.ds(i, 1)], in0=y.rearrange("p (o s) -> p o s", o=1),
                                         scalar=g_conv[:, bass.ds(i, 1)], in1=conv_hi[:, bass.ds(i, 1)].bitcast(F32),
                                         op0=ALU.mult, op1=ALU.subtract).then_inc(conv_lo_made, 1)
            ch.n = first + 3 * CI
            split_lo(3 * CI + 3, 0)
            for m in range(3):
                dve.wait_ge(lat_squared, m + 1)
                dve.tensor_copy(tmp[m], s_bank[m]).then_inc(lat_copied, 1)

            def rope(out, src):
                ch.done(dve.tensor_tensor(out, src[0:ROPE], cossin[0:ROPE], ALU.mult))
                ch.done(dve.tensor_tensor(rope_t, src[ROPE:P], cossin[ROPE:P], ALU.mult))
                return dve.tensor_tensor(out, out, rope_t, ALU.add)

            dve.wait_ge(tile_done, 3 * CI + 4)
            rope(k_pe, s_bank[0]).then_inc(kpe_made, 1)
            dve.wait_ge(lat_copied, 3)
            dve.wait_ge(lat_std, 1)
            ch.done(dve.reciprocal(r_kv, r_kv))
            dve.scalar_tensor_tensor(out=ckvn, in0=ckvn, scalar=g_kv[:, 0:1], in1=r_kv,
                                     op0=ALU.mult, op1=ALU.mult).then_inc(lat_normed, 1)
            dve.wait_ge(lat_std, 2)
            ch.done(dve.reciprocal(r_q, r_q))
            for k in range(2):
                dve.scalar_tensor_tensor(out=cqn[:, k], in0=cqn[:, k], scalar=g_q[:, k:k + 1], in1=r_q,
                                         op0=ALU.mult, op1=ALU.mult).then_inc(lat_normed, 1)
            dve.wait_ge(lat_normed, 3)
            first = ch.n
            HEAD_STEPS = 2 + 3 * T
            with dve.Fori(0, N_HEADS) as h:
                ch.n = h * HEAD_STEPS + first

                def neg_max(i):
                    b, n = i % 2, (i + 1) * P
                    dve.wait_ge(scores_done, h * T + i + 1)
                    if i >= 2:
                        dve.wait_ge(prob_made, h * T + i - 1)
                    ch.done(dve.tensor_tensor(s_bank[b][:, i * P:n], s_bank[b][:, i * P:n], mask[:], ALU.add))
                    ch.done(dve.tensor_reduce(negm[:, 2 + b:3 + b], s_bank[b][:, 0:n], AX.X, ALU.max))
                    dve.tensor_scalar(negm[:, b:b + 1], negm[:, 2 + b:3 + b], -SCALE, None, ALU.mult).then_inc(negmax_made, 1)

                def turned_o(i):
                    b = i % 2
                    dve.wait_ge(ot_hi_made, h * T + i + 1)
                    dve.scalar_tensor_tensor(out=att_lo[:, bass.ds(h, 1), i * P:(i + 1) * P],
                                             in0=psum[:, 7:8, 0:P], scalar=g_att[:, bass.ds(h, 1)],
                                             in1=att_hi[:, bass.ds(h, 1), i * P:(i + 1) * P].bitcast(F32),
                                             op0=ALU.mult, op1=ALU.subtract).then_inc(ot_lo_made, 1)

                dve.wait_ge(q_done, h * 4 + 2)
                rope(q_pe, s_bank[1]).then_inc(qpe_made, 1)
                def scale_o(i):
                    b, c = i % 2, i % 4
                    dve.wait_ge(o_done, h * T + i + 1)
                    if i >= 2:
                        dve.wait_ge(o_turned, h * T + i - 1)
                        dve.wait_ge(o_squared, h * T + i - 1)
                    ch.done(dve.reciprocal(psum_p[:, 4 + c:5 + c], psum_p[:, c:c + 1]))
                    dve.tensor_scalar(o_sb[:, b], psum[:, 6, 0:P], psum_p[:, 4 + c:5 + c], None,
                                      ALU.mult).then_inc(o_scaled, 1)

                neg_max(0)
                for i in range(T):
                    if i + 1 < T:
                        neg_max(i + 1)
                    if i >= 1:
                        scale_o(i - 1)
                    if i >= 2:
                        turned_o(i - 2)
                scale_o(T - 1)
                turned_o(T - 2)
                turned_o(T - 1)

        @block.tensor
        def _(pe):
            ident, ones = keep["ident"], keep["ones"]
            pe.wait_ge(consts_made, CONSTS)

            def turn_x(t, b, reused):
                pe.wait_ge(xn_made, t + 1)
                for q in range(2):
                    if reused:
                        pe.wait_ge(xt_lo_made, t * 2 + (q - 3))
                    for k in range(4):
                        mm = pe.transpose(psum[:, 2 * b + q, k * P:(k + 1) * P],
                                          xn[:, b, (4 * q + k) * P:(4 * q + k + 1) * P], ident[:])
                    mm.then_inc(x_turned, 1)

            turn_x(0, 0, False)
            turn_x(1, 1, False)
            with pe.Fori(1, T // 2) as pair:
                for b in range(2):
                    turn_x(pair * 2 + b, b, True)
            pe.wait_ge(xt_lo_made, 2 * T)

            def column_tile(n, r):
                pe.wait_ge(ws_lo_made, n + 1)
                for j in range(HALF):
                    cols = slice(j * BANK, (j + 1) * BANK)
                    for k in range(KD):
                        mm = split_mm(pe, psum[:, 2 * r + j], ws_k[:, r, 0, k], ws_k[:, r, 1, k],
                                      xh[:, k, cols], xl[:, k, cols], k == 0, k == KD - 1)
                mm.then_inc(tile_done, 1)

            with pe.Fori(0, CI) as i:
                with pe.If(i > 0):
                    pe.wait_ge(c_copied, i)
                    pe.sem_inc(pe_passed, 1)
                column_tile(i * 3, 0)
                with pe.If(i > 0):
                    pe.wait_ge(u_made, i)
                    pe.sem_inc(pe_passed, 1)
                column_tile(i * 3 + 1, 1)
                with pe.If(i > 0):
                    pe.wait_ge(y_made, i)
                    pe.sem_inc(pe_passed, 1)
                column_tile(i * 3 + 2, 2)
            pe.wait_ge(c_copied, CI)
            column_tile(3 * CI, 0)
            pe.wait_ge(u_made, CI)
            column_tile(3 * CI + 1, 1)
            pe.wait_ge(y_made, CI)
            column_tile(3 * CI + 2, 2)
            pe.wait_ge(lat_squared, 1)
            pe.wait_ge(lat_copied, 1)
            column_tile(3 * CI + 3, 0)
            pe.wait_ge(lat_squared, 3)
            pe.wait_ge(lat_copied, 3)
            for j in range(HALF):
                mm = pe.matmul(psum[:, 4 + j], ones[:], sq_kv[:, j * BANK:(j + 1) * BANK], start=True, stop=True)
            mm.then_inc(lat_ss_done, 1)
            for j in range(HALF):
                for k in range(2):
                    mm = pe.matmul(psum[:, 2 + j], ones[:], sq_cq[:, k, j * BANK:(j + 1) * BANK],
                                   start=(k == 0), stop=(k == 1))
            mm.then_inc(lat_ss_done, 1)
            pe.wait_ge(y_squared, CI)
            for t in range(T):
                for i in range(CI):
                    mm = pe.matmul(psum[:, 6, t:t + 1], sq_conv[:, i, t * P:(t + 1) * P], ones[:, 0:1],
                                   start=(i == 0), stop=(i == CI - 1))
            mm.then_inc(conv_ss_done, 1)
            pe.wait_ge(ukv_loaded, 16)
            pe.wait_ge(lat_normed, 1)
            for h in range(N_HEADS):
                if h == 0:
                    pe.wait_ge(kpe_made, 1)
                elif h == 1:
                    pe.wait_ge(lat_std, 2)
                else:
                    pe.wait_ge(k_copied, h - 1)
                for j in range(HALF):
                    mm = pe.matmul(psum[:, 2 * (h % 2) + j], w_ukv[:, 2 * h * P:2 * h * P + P],
                                   ckvn[:, j * BANK:(j + 1) * BANK], start=True, stop=True)
                mm.then_inc(k_done, 1)
            w_v = w_ukv.rearrange("p (h z c) -> p h z c", h=N_HEADS, z=2)[:, :, 1]
            for t in range(T):
                if t >= 2:
                    pe.wait_ge(v_copied, t - 1)
                pe.matmul(psum[:, 4 + t % 2].rearrange("p (h c) -> p h c", h=N_HEADS), ckvn[:, t * P:(t + 1) * P], w_v,
                          start=True, stop=True).then_inc(v_done, 1)
            pe.wait_ge(k_copied, N_HEADS)
            pe.wait_ge(v_copied, T)
            pe.wait_ge(conv_ss_copied, 1)
            pe.wait_ge(lat_normed, 3)

            with pe.Fori(0, N_HEADS) as h:
                with pe.If(h > 0):
                    pe.wait_ge(prob_made, h * T)
                    pe.sem_inc(pe_passed, 1)
                pe.wait_ge(wqh_loaded, h * 48 + 48)
                for z in (1, 0):
                    for j in range(HALF):
                        for k in range(2):
                            mm = pe.matmul(psum[:, 2 * z + j], w_qh[:, k, z * P:(z + 1) * P],
                                           cqn[:, k, j * BANK:(j + 1) * BANK], start=(k == 0), stop=(k == 1))
                        mm.then_inc(q_done, 1)

                def scores(i):
                    b, n = i % 2, (i + 1) * P
                    if i >= 2:
                        pe.wait_ge(prob_made, h * T + i - 1)
                    for c0 in range(0, n, BANK):
                        w = min(BANK, n - c0)
                        pe.matmul(s_bank[b][:, c0:c0 + w], q_nope[:, i * P:n],
                                  keys[:, bass.ds(h, 1), c0:c0 + w], start=True, stop=False)
                        mm = pe.matmul(s_bank[b][:, c0:c0 + w], q_pe[:, i * P:n], k_pe[:, c0:c0 + w],
                                       start=False, stop=True)
                    mm.then_inc(scores_done, 1)

                def turn_o(i):
                    b = i % 2
                    pe.wait_ge(o_scaled, h * T + i + 1)
                    if i >= 1:
                        pe.wait_ge(ot_lo_made, h * T + i)
                    pe.transpose(psum[:, 7, 0:P], o_sb[:, b], ident[:]).then_inc(o_turned, 1)

                def weigh(i):
                    pe.wait_ge(pt_made, h * T + i + 1)
                    if i >= 1:
                        pe.wait_ge(o_scaled, h * T + i)
                    for kb in range(i + 1):
                        mm = pe.matmul(psum[:, 6, 0:P], pt[i % 2][:, kb * P:(kb + 1) * P],
                                       values[:, kb, bass.ds(h * P, P)], start=(kb == 0), stop=(kb == i))
                    mm.then_inc(o_done, 1)

                with pe.If(h > 0):
                    pe.wait_ge(ot_lo_made, h * T)
                    pe.wait_ge(o_squared, h * T)
                    pe.sem_inc(pe_passed, 1)
                pe.wait_ge(qn_copied, h + 1)
                pe.wait_ge(qpe_made, h + 1)
                scores(0)
                for i in range(T):
                    if i + 1 < T:
                        scores(i + 1)
                    pe.wait_ge(prob_made, h * T + i + 1)
                    if i >= 1:
                        pe.wait_ge(pt_made, h * T + i)
                    for kb in range(i + 1):
                        mm = pe.transpose(turn_ps[:, kb * P:(kb + 1) * P], prob[:, i % 2, kb * P:(kb + 1) * P], ident[:])
                    mm.then_inc(prob_turned, 1)
                    if i >= 1:
                        weigh(i - 1)
                    if i >= 2:
                        turn_o(i - 2)
                weigh(T - 1)
                turn_o(T - 2)
                turn_o(T - 1)


def route_phase(nc, dram, keep):
    x = dram["x"]
    S, D = x.shape[1], x.shape[2]
    T, KD = S // P, D // P
    E = dram["w_router"].shape[2]
    BLOCKS = S // P
    GROUPS = (BLOCKS + 1) // 2
    NBLK = blocks_bound(S, E)
    NC = D // BANK
    HALF_C = 4

    att = [keep["wide"][:, z, 0:4 * S].rearrange("p (k s) -> p k s", k=4) for z in range(2)]
    conv = [keep["conv"][:, z] for z in range(2)]
    wo0 = [keep["wide"][:, z, 4 * S:8 * S].rearrange("p (k n) -> p k n", k=KD) for z in range(2)]

    with ExitStack() as ctx:
        def sb(name, shape, dt=F32):
            return ctx.enter_context(nc.sbuf_tensor(name, shape, dt))

        sems = []

        def sem(name):
            sems.append(nc.alloc_semaphore(name=name))
            return sems[-1]

        wo1_t = sb("wo1", [P, 2, KD, BANK], F32R)
        wo = [wo0, [wo1_t[:, z] for z in range(2)]]
        raw = sb("wo_raw", [P, KD, BANK])
        h = sb("h", [P, T, D])
        g_moe = sb("g_moe", [P, D])
        hn = sb("hn", [P, 2, D])
        hnt = raw[:, 4:8].rearrange("p k n -> p (k n)").rearrange("p (b k m) -> p b k m", b=2, k=KD)
        w_r = raw[:, 0, 0:KD * E].rearrange("p (k e) -> p k e", k=KD)
        gt = raw[:, 1, 0:2 * P].rearrange("p (z m) -> p z m", z=2)
        zero_t = sb("zero_t", [P, NBLK])
        zeros = zero_t[:]
        b_r = sb("b_r", [P, E])
        b2r = g_moe
        b1raw = raw[0:2 * E].rearrange("p k n -> p (k n)")[:, 0:2 * D]
        small = sb("small", [P, 24 * 32])
        bf = sb("bf", [P, 12 * 32 + 2 * P], BF16)
        idx_u = sb("idx_u", [P, T, 8], U32)
        iota_i = sb("iota_i", [P, 160], I32)
        tab_i = sb("tab_i", [P, 8], I32)
        big = hn[:].rearrange("p b d -> p (b d)")
        one_hot = big[:, 0:T * TOP_K * E].rearrange("p (a e) -> p a e", e=E)
        prod = big[:, D:D + T * TOP_K * E].rearrange("p (a e) -> p a e", e=E)
        psum = ctx.enter_context(nc.psum_tensor("route_psum", [P, 8, BANK], F32))

        at = [0]

        def cut(n):
            at[0] += n
            return small[:, at[0] - n:at[0]]

        r_mix = cut(2 * T)
        ssh = cut(3 * T)
        logits = cut(T * E).rearrange("p (t e) -> p t e", t=T)
        top = cut(T * 8).rearrange("p (t k) -> p t k", t=T)
        idx_f = cut(T * TOP_K)
        g_sum = cut(2 * T)
        slot_f = cut(T * TOP_K)
        tok_id = cut(T)
        counts, ng, gend, le, oh, nb, bend = (cut(E) for _ in range(7))
        gcol = cut(16)
        iota_e = cut(E)
        upper, ones_b = bf[:, 0:P], bf[:, P:2 * P]
        m_b = bf[:, 2 * P:2 * P + T * E].rearrange("p (t e) -> p t e", t=T)
        has2_b = bf[:, 2 * P + T * E:2 * P + T * E + 1]
        gd = hnt[:, 0].rearrange("p k m -> p (k m)")[:, 0:T * E].rearrange("p (t e) -> p t e", t=T)
        pos_e = hnt[:, 1].rearrange("p k m -> p (k m)")[:, 0:T * E].rearrange("p (t e) -> p t e", t=T)
        tokens = hnt[0:NBLK, 0].rearrange("p k m -> p (k m)")[:, 512:512 + P]
        oh2 = hnt[:, 0].rearrange("p k m -> p (k m)")[:, 768:768 + 2 * E]

        h_loaded = sem("h_loaded")
        raw_loaded = [sem(f"wo_raw_loaded{z}") for z in range(2)]
        route_par_loaded = sem("route_par_loaded")
        b1_loaded = sem("b1_loaded")
        route_consts = sem("route_consts")
        zeroed = sem("zeroed")
        r_std = sem("r_std")
        wo_hi_made = sem("wo_hi_made")
        wo_lo_made = sem("wo_lo_made")
        wo_done = sem("wo_done")
        h_made = sem("h_made")
        h_squared = sem("h_squared")
        h_std = sem("h_std")
        hn_made = sem("hn_made")
        hn_stored = [sem(f"hn_stored{b}") for b in range(2)]
        hn_turned = sem("hn_turned")
        hnt_copied = sem("hnt_copied")
        hnt_copied2 = sem("hnt_copied2")
        logits_done = sem("logits_done")
        gates_shifted = sem("gates_shifted")
        gates_exp = sem("gates_exp")
        marks_made = sem("marks_made")
        ranks_done = sem("ranks_done")
        slots_made = sem("slots_made")
        gd_made = sem("gd_made")
        gd_turned = sem("gd_turned")
        gt_copied = sem("gt_copied")
        b2_done = sem("b2_done")
        h2_made = sem("h2_made")
        h2_stored = sem("h2_stored")
        scattered = sem("scattered")
        tokens_loaded = sem("tokens_loaded")
        tokens_turned = sem("tokens_turned")
        has2_made = sem("has2_made")
        before_done = sem("before_done")
        table_made = sem("table_made")
        table_stored = sem("table_stored")
        table_loaded = sem("table_loaded")
        oh_made = sem("oh_made")
        oh_turned = sem("oh_turned")
        b1_hi = sem("b1_hi")
        b1_lo = sem("b1_lo")
        wr_loaded = sem("wr_loaded")
        b2_loaded = sem("b2_loaded")
        dve_passed = sem("dve_passed2")
        dve_step = sem("dve_step2")

        w_o3 = dram["w_o"][0].rearrange("(k p) n -> p k n", p=P)
        x_rows = x[0].rearrange("(t p) d -> p t d", p=P)
        hn_rows = dram["hn_rows"].rearrange("(t p) d -> p t d", p=P)
        h_rows = dram["h_rows"].rearrange("(t p) d -> p t d", p=P)
        row_tok = dram["row_tok"]

        block = ctx.enter_context(phase_block(nc, sems))

        @block.sync
        def _(sp):
            for z in range(2):
                sp.dma_start(raw[:, 4 * z:4 * z + 4], w_o3[:, 4 * z:4 * z + 4, 0:BANK]).then_inc(raw_loaded[z], 16)
            sp.dma_start(h[:], x_rows).then_inc(h_loaded, 16)
            sp.dma_start(g_moe[:], dram["moe_norm"][0:1, :].partition_broadcast(P)).then_inc(route_par_loaded, 16)
            sp.dma_start(b_r[:], dram["b_router"][0:1, :].partition_broadcast(P)).then_inc(route_par_loaded, 16)
            sp.wait_ge(wo_lo_made, 2)
            for z in range(2):
                sp.dma_start(raw[:, 4 * z:4 * z + 4], w_o3[:, 4 * z:4 * z + 4, BANK:2 * BANK]).then_inc(raw_loaded[z], 16)
            sp.wait_ge(route_consts, 1)
            sp.dma_start(row_tok.rearrange("(p n) o -> p (n o)", p=P), zeros).then_inc(zeroed, 16)
            sp.wait_ge(wo_lo_made, 4)
            for z in range(2):
                sp.dma_start(b1raw[z * E:(z + 1) * E], dram["b1"][0]).then_inc(b1_loaded, 16)
            sp.wait_ge(b1_lo, 1)
            sp.dma_start(w_r, dram["w_router"][0].rearrange("(k p) e -> p k e", p=P)).then_inc(wr_loaded, 16)
            with sp.Fori(0, T // 2) as pair:
                for b in range(2):
                    t = pair * 2 + b
                    sp.wait_ge(hn_made, t + 1)
                    sp.dma_start(hn_rows[:, bass.ds(t, 1)], hn[:, b:b + 1]).then_inc(hn_stored[b], 16)
            for j in range(P // E):
                sp.dma_start(b2r[j * E:(j + 1) * E], dram["b2"][0]).then_inc(b2_loaded, 16)
            sp.wait_ge(scattered, 16 * T * TOP_K)
            sp.dma_start(tokens, row_tok.rearrange("(b c) o -> b (c o)", c=P)).then_inc(tokens_loaded, 16)
            sp.wait_ge(table_made, 1)
            sp.dma_start(dram["table"], tab_i[:]).then_inc(table_stored, 16)
            sp.wait_ge(table_stored, 16)
            sp.dma_start(keep["tab"][:], dram["table"][0:P // 2].rearrange("(o g) c -> o (g c)", o=1)).then_inc(table_loaded, 16)
            with sp.Fori(0, T) as t:
                sp.wait_ge(h2_made, t + 1)
                sp.dma_start(h_rows[:, bass.ds(t, 1)], h[:, bass.ds(t, 1)]).then_inc(h2_stored, 16)
            sp.wait_ge(h2_stored, 16 * T)
            sp.wait_ge(table_loaded, 16)
            for b in range(2):
                sp.wait_ge(hn_stored[b], 16 * (T // 2))

        @block.gpsimd
        def _(pool):
            pool.memset(zeros, 0.0).then_inc(route_consts, 1)
            pool.memset(upper, 1.0).then_inc(route_consts, 1)
            pool.memset(ones_b, 1.0).then_inc(route_consts, 1)
            pool.iota(iota_i[:, 0:T], [[P, T]], base=0, channel_multiplier=1).then_inc(route_consts, 1)
            pool.iota(iota_i[:, 32:32 + E], [[1, E]], base=0, channel_multiplier=0).then_inc(route_consts, 1)
            pool.wait_ge(route_consts, 2)
            pool.affine_select(out=upper, in_=upper, compare_op=ALU.is_gt, fill=0.0, base=0,
                               pattern=[[1, P]], channel_multiplier=-1).then_inc(route_consts, 1)
            pool.wait_ge(zeroed, 16)
            pool.wait_ge(slots_made, 1)
            for t in range(T):
                for k in range(TOP_K):
                    pool.indirect_dma_start(out=row_tok, out_offset=bass.IndirectOffsetOnAxis(ap=keep["slots"][:, t, k:k + 1], axis=0),
                                            in_=tok_id[:, t:t + 1], in_offset=None).then_inc(scattered, 16)
            pool.wait_ge(scattered, 16 * T * TOP_K)

        @block.scalar
        def _(act):
            act.wait_ge(r_std, 1)
            act.activation(r_mix, r_mix, ACT.Sqrt, scale=1.0 / (4 * P), bias=keep["eps"][:, 0:1]).then_inc(r_std, 1)
            for c in range(NC):
                for z in range(2):
                    act.wait_ge(raw_loaded[z], 16 * (c + 1))
                    act.activation(wo[c][0][:, 4 * z:4 * z + 4], raw[:, 4 * z:4 * z + 4], ACT.Copy).then_inc(wo_hi_made, 1)
            act.wait_ge(b1_loaded, 32)
            act.activation(keep["b1s"][:], b1raw, ACT.Copy).then_inc(b1_hi, 1)
            act.wait_ge(zeroed, 16)
            for t in range(T):
                act.wait_ge(h_made, T + t + 1)
                if t >= 1:
                    act.wait_ge(h_squared, t)
                act.activation(hnt[:, 0].rearrange("p k m -> p (k m)"), h[:, t], ACT.Square,
                               accum_out=ssh[:, t:t + 1]).then_inc(h_squared, 1)
            act.wait_ge(h_squared, T)
            act.activation(ssh[:, T:2 * T], ssh[:, 0:T], ACT.Sqrt, scale=1.0 / D, bias=keep["eps"][:, 0:1]).then_inc(h_std, 1)
            with act.Fori(0, T // 2) as pair:
                for b in range(2):
                    act.wait_ge(hn_turned, pair * 4 + (2 * b + 1))
                    act.activation(hnt[:, b, 0:4], psum[:, 2 * b].rearrange("p (k m) -> p k m", k=4), ACT.Copy).then_inc(hnt_copied, 1)
            act.wait_ge(gates_shifted, 1)
            act.activation(top[:, :, 0:TOP_K], top[:, :, 0:TOP_K], ACT.Exp).then_inc(gates_exp, 1)

        @block.vector
        def _(dve):
            ch = Chain(dve, dve_step)
            ch.done(dve.tensor_reduce(r_mix[:, 0:T], keep["ss_att"][:], AX.X, ALU.add))
            dve.tensor_copy(r_mix[:, T:2 * T], keep["ss_conv"][:]).then_inc(r_std, 1)
            for c in range(NC):
                for z in range(2):
                    dve.wait_ge(wo_hi_made, 2 * c + z + 1)
                    dve.tensor_tensor(wo[c][1][:, 4 * z:4 * z + 4], raw[:, 4 * z:4 * z + 4],
                                          wo[c][0][:, 4 * z:4 * z + 4].bitcast(F32), ALU.subtract).then_inc(wo_lo_made, 1)
            dve.wait_ge(r_std, 2)
            ch.done(dve.reciprocal(r_mix, r_mix))
            dve.wait_ge(h_loaded, 16)
            for c in range(NC):
                for t in range(T):
                    b = t % 4
                    hc = h[:, t, c * BANK:(c + 1) * BANK]
                    dve.wait_ge(wo_done, c * T + t + 1)
                    ch.done(dve.scalar_tensor_tensor(out=hc, in0=psum[:, 2 * b], scalar=r_mix[:, t:t + 1], in1=hc,
                                                     op0=ALU.mult, op1=ALU.add))
                    dve.scalar_tensor_tensor(out=hc, in0=psum[:, 2 * b + 1], scalar=r_mix[:, T + t:T + t + 1], in1=hc,
                                             op0=ALU.mult, op1=ALU.add).then_inc(h_made, 1)
            dve.wait_ge(b1_hi, 1)
            dve.tensor_tensor(keep["b1s"][E:2 * E], b1raw[E:2 * E], keep["b1s"][E:2 * E].bitcast(F32), ALU.subtract).then_inc(b1_lo, 1)
            dve.wait_ge(route_consts, 6)
            ch.done(dve.tensor_copy(tok_id, iota_i[:, 0:T]))
            ch.done(dve.tensor_copy(iota_e, iota_i[:, 32:32 + E]))
            dve.wait_ge(route_par_loaded, 32)
            dve.wait_ge(h_std, 1)
            ch.done(dve.reciprocal(ssh[:, 2 * T:3 * T], ssh[:, T:2 * T]))
            def norm_rows(t, b):
                dve.scalar_tensor_tensor(out=hn[:, b:b + 1], in0=h[:, bass.ds(t, 1)], scalar=ssh[:, bass.ds(t + 2 * T, 1)],
                                         in1=g_moe[:].rearrange("p (o d) -> p o d", o=1),
                                         op0=ALU.mult, op1=ALU.mult).then_inc(hn_made, 1)

            def copy_turned(t, b):
                dve.wait_ge(hn_turned, t * 2 + 2)
                dve.tensor_copy(hnt[:, b, 4:8], psum[:, 2 * b + 1].rearrange("p (k m) -> p k m", k=4)).then_inc(hnt_copied2, 1)

            norm_rows(0, 0)
            with dve.Fori(0, T // 2 - 1) as pair:
                with dve.If(pair > 0):
                    dve.wait_ge(hn_stored[1], pair * 16)
                    dve.sem_inc(dve_passed, 1)
                norm_rows(pair * 2 + 1, 1)
                copy_turned(pair * 2, 0)
                dve.wait_ge(hn_stored[0], pair * 16 + 16)
                norm_rows(pair * 2 + 2, 0)
                copy_turned(pair * 2 + 1, 1)
            dve.wait_ge(hn_stored[1], 16 * (T // 2 - 1))
            norm_rows(T - 1, 1)
            copy_turned(T - 2, 0)
            copy_turned(T - 1, 1)
            dve.wait_ge(logits_done, T)
            ch.done(dve.tensor_tensor(logits, psum[:, 4, 0:T * E].rearrange("p (t e) -> p t e", t=T),
                                      b_r[:].rearrange("p (o e) -> p o e", o=1).broadcast_to([P, T, E]), ALU.add))
            for t in range(T):
                dve.max(top[:, t], logits[:, t]).then_inc(dve_step, 1)
            ch.n = ch.n + T
            dve.wait_ge(dve_step, ch.n)
            for t in range(T):
                dve.max_index(idx_u[:, t], top[:, t], logits[:, t]).then_inc(dve_step, 1)
            ch.n = ch.n + T
            dve.wait_ge(dve_step, ch.n)
            ch.done(dve.tensor_copy(idx_f.rearrange("p (t k) -> p t k", t=T), idx_u[:, :, 0:TOP_K]))
            ch.done(dve.tensor_copy(g_sum[:, 0:T], top[:, :, 0]))
            dve.tensor_tensor(top[:, :, 0:TOP_K], top[:, :, 0:TOP_K],
                              g_sum[:, 0:T].rearrange("p (t o) -> p t o", o=1).broadcast_to([P, T, TOP_K]),
                              ALU.subtract).then_inc(gates_shifted, 1)
            for b in range(2):
                dve.wait_ge(hn_stored[b], 16 * (T // 2))
            dve.wait_ge(hn_turned, 2 * T)
            ch.done(dve.tensor_tensor(one_hot, iota_e.rearrange("p (o e) -> p o e", o=1).broadcast_to([P, T * TOP_K, E]),
                                      idx_f.rearrange("p (a o) -> p a o", o=1).broadcast_to([P, T * TOP_K, E]), ALU.is_equal))
            by_tile = big[:, 0:T * TOP_K * E].rearrange("p (t k e) -> p t e k", t=T, k=TOP_K)
            prod_by_tile = big[:, D:D + T * TOP_K * E].rearrange("p (t k e) -> p t e k", t=T, k=TOP_K)
            with nc.allow_low_precision(reason="0 and 1 are exact"):
                dve.tensor_reduce(m_b, by_tile, AX.X, ALU.add).then_inc(marks_made, 1)
            dve.wait_ge(gates_exp, 1)
            ch.done(dve.tensor_reduce(g_sum[:, 0:T], top[:, :, 0:TOP_K], AX.X, ALU.add))
            ch.done(dve.reciprocal(g_sum[:, T:2 * T], g_sum[:, 0:T]))
            ch.done(dve.tensor_tensor(keep["gates"][:], top[:, :, 0:TOP_K],
                                      g_sum[:, T:2 * T].rearrange("p (t o) -> p t o", o=1).broadcast_to([P, T, TOP_K]), ALU.mult))
            dve.wait_ge(ranks_done, 1)
            ch.done(dve.tensor_copy(counts, psum[:, 6, 0:E]))
            ch.done(dve.tensor_scalar(nb, counts, 0.0, None, ALU.is_gt))
            for m in range(1, BLOCKS):
                ch.done(dve.scalar_tensor_tensor(out=nb, in0=counts, scalar=float(P * m), in1=nb, op0=ALU.is_gt, op1=ALU.add))
            ch.done(dve.tensor_tensor_scan(bend, keep["ones"][:, 0:E], nb, 0.0, ALU.mult, ALU.add))
            ch.done(dve.tensor_tensor(nb, bend, nb, ALU.subtract))
            ch.done(dve.scalar_tensor_tensor(out=pos_e, in0=nb.rearrange("p (o e) -> p o e", o=1).broadcast_to([P, T, E]),
                                             scalar=float(P), in1=psum[:, 5, 0:T * E].rearrange("p (t e) -> p t e", t=T),
                                             op0=ALU.mult, op1=ALU.add))
            prod4 = big[:, D:D + T * TOP_K * E].rearrange("p (t k e) -> p t k e", t=T, k=TOP_K)
            hot4 = big[:, 0:T * TOP_K * E].rearrange("p (t k e) -> p t k e", t=T, k=TOP_K)
            for k in range(TOP_K):
                i = dve.tensor_tensor(prod4[:, :, k], hot4[:, :, k], pos_e, ALU.mult)
                i.then_inc(dve_step, 1)
            ch.n = ch.n + TOP_K
            dve.wait_ge(dve_step, ch.n)
            ch.done(dve.tensor_reduce(slot_f, prod, AX.X, ALU.add))
            dve.tensor_copy(keep["slots"][:], slot_f.rearrange("p (t k) -> p t k", t=T)).then_inc(slots_made, 1)
            ch.done(dve.tensor_tensor(prod, one_hot, keep["gates"][:].rearrange("p t k -> p (t k)").rearrange("p (a o) -> p a o", o=1)
                                      .broadcast_to([P, T * TOP_K, E]), ALU.mult))
            dve.tensor_reduce(gd, prod_by_tile, AX.X, ALU.add).then_inc(gd_made, 1)
            ch.done(dve.tensor_scalar(ng, counts, 0.0, None, ALU.is_gt))
            for m in range(1, GROUPS):
                ch.done(dve.scalar_tensor_tensor(out=ng, in0=counts, scalar=float(2 * P * m), in1=ng, op0=ALU.is_gt, op1=ALU.add))
            ch.done(dve.tensor_tensor_scan(gend, keep["ones"][:, 0:E], ng, 0.0, ALU.mult, ALU.add))
            eid, gst, cnt, has2, valid, blk = (gcol[:, i:i + 1] for i in range(6))
            ch.done(dve.tensor_scalar(le, gend, tok_id[:, 0:1], None, ALU.is_le))
            ch.done(dve.tensor_reduce(eid, le, AX.X, ALU.add))
            ch.done(dve.tensor_tensor(le, le, ng, ALU.mult))
            ch.done(dve.tensor_reduce(gst, le, AX.X, ALU.add))
            ch.done(dve.tensor_scalar(oh, iota_e, eid, None, ALU.is_equal))
            ch.done(dve.tensor_tensor(le, oh, counts, ALU.mult))
            ch.done(dve.tensor_reduce(cnt, le, AX.X, ALU.add))
            ch.done(dve.tensor_tensor(gst, tok_id[:, 0:1], gst, ALU.subtract))
            ch.done(dve.scalar_tensor_tensor(out=cnt, in0=gst, scalar=-2.0 * P, in1=cnt, op0=ALU.mult, op1=ALU.add))
            ch.done(dve.tensor_scalar(has2, cnt, float(P), None, ALU.is_gt))
            ch.done(dve.tensor_scalar(valid, eid, float(E), None, ALU.is_lt))
            dve.tensor_copy(has2_b, has2).then_inc(has2_made, 1)
            ch.done(dve.tensor_tensor(le, oh, nb, ALU.mult))
            ch.done(dve.tensor_reduce(blk, le, AX.X, ALU.add))
            ch.done(dve.tensor_scalar(eid, eid, float(E - 1), None, ALU.min))
            ch.done(dve.scalar_tensor_tensor(out=blk, in0=gst, scalar=2.0, in1=blk, op0=ALU.mult, op1=ALU.add))
            ch.done(dve.tensor_scalar(blk, blk, float(NBLK - 2), None, ALU.min))
            for i, c in enumerate([eid, blk, has2, valid]):
                ch.done(dve.tensor_copy(tab_i[:, i:i + 1], c))
            dve.wait_ge(before_done, 1)
            ch.done(dve.tensor_copy(tab_i[:, 4:6], psum[:, 7, 0:2]))
            ch.done(dve.tensor_copy(tab_i[:, 6:7], gend[:, E - 1:E]))
            dve.memset(tab_i[:, 7:8], 0).then_inc(table_made, 1)
            ch.done(dve.tensor_copy(oh2[:, 0:E], oh))
            dve.tensor_copy(oh2[:, E:2 * E], oh).then_inc(oh_made, 1)
            for z in range(2):
                dve.wait_ge(gd_turned, z + 1)
                dve.tensor_copy(gt[:, z], psum[:, z, 0:P]).then_inc(gt_copied, 1)
            dve.wait_ge(oh_turned, 1)
            ch.done(dve.tensor_copy(keep["sel_all"][:], psum[0:2 * E, 7, P:2 * P]))
            for t in range(T):
                dve.wait_ge(b2_done, t + 1)
                dve.tensor_tensor(h[:, t], psum[:, 2 * (t % 2):2 * (t % 2) + 2].rearrange("p b n -> p (b n)"), h[:, t],
                                  ALU.add).then_inc(h2_made, 1)
            dve.wait_ge(tokens_turned, 1)
            ch.done(dve.tensor_copy(keep["idx"][:], psum[:, 5, 0:NBLK]))

        @block.tensor
        def _(pe):
            for c in range(NC):
                for t in range(T):
                    b = t % 4
                    cols = slice(t * P, (t + 1) * P)
                    if c * T + t >= 4:
                        pe.wait_ge(h_made, c * T + t - 3)
                    if t == 0:
                        pe.wait_ge(wo_lo_made, 2 * c + 1)
                    for k in range(HALF_C):
                        split_mm(pe, psum[:, 2 * b], att[0][:, k, cols], att[1][:, k, cols],
                                 wo[c][0][:, k], wo[c][1][:, k], k == 0, k == HALF_C - 1)
                    if t == 0:
                        pe.wait_ge(wo_lo_made, 2 * c + 2)
                    for k in range(HALF_C):
                        mm = split_mm(pe, psum[:, 2 * b + 1], conv[0][:, k, cols], conv[1][:, k, cols],
                                      wo[c][0][:, HALF_C + k], wo[c][1][:, HALF_C + k], k == 0, k == HALF_C - 1)
                    mm.then_inc(wo_done, 1)
            pe.wait_ge(h_made, NC * T)
            pe.wait_ge(wr_loaded, 16)
            ident = keep["ident"]
            def turn_rows(t, b):
                pe.wait_ge(hn_made, t + 1)
                for q in range(2):
                    for k in range(4):
                        mm = pe.transpose(psum[:, 2 * b + q, k * P:(k + 1) * P],
                                          hn[:, b, (4 * q + k) * P:(4 * q + k + 1) * P], ident[:])
                    mm.then_inc(hn_turned, 1)

            def router(t, b):
                pe.wait_ge(hnt_copied, t + 1)
                pe.wait_ge(hnt_copied2, t + 1)
                for k in range(KD):
                    mm = pe.matmul(psum[:, 4, bass.ds(t * E, E)], hnt[:, b, k], w_r[:, k], start=(k == 0), stop=(k == KD - 1))
                mm.then_inc(logits_done, 1)

            turn_rows(0, 0)
            with pe.Fori(0, T // 2 - 1) as pair:
                for b in range(2):
                    turn_rows(pair * 2 + b + 1, 1 - b)
                    router(pair * 2 + b, b)
            turn_rows(T - 1, 1)
            router(T - 2, 0)
            router(T - 1, 1)
            pe.wait_ge(marks_made, 1)
            for t in range(T):
                for u in range(t):
                    pe.matmul(psum[:, 5, t * E:(t + 1) * E], ones_b, m_b[:, u], start=(u == 0), stop=False)
                pe.matmul(psum[:, 5, t * E:(t + 1) * E], upper, m_b[:, t], start=(t == 0), stop=True)
            for t in range(T):
                mm = pe.matmul(psum[:, 6, 0:E], ones_b, m_b[:, t], start=(t == 0), stop=(t == T - 1))
            mm.then_inc(ranks_done, 1)
            pe.wait_ge(has2_made, 1)
            pe.matmul(psum[:, 7, 0:1], upper, has2_b, start=True, stop=True)
            pe.matmul(psum[:, 7, 1:2], ones_b, has2_b, start=True, stop=True).then_inc(before_done, 1)
            pe.wait_ge(gd_made, 1)
            for z in range(2):
                pe.transpose(psum[:, z, 0:P], gd[:, 4 * z:4 * z + 4].rearrange("p t e -> p (t e)"), ident[:]).then_inc(gd_turned, 1)
            pe.wait_ge(oh_made, 1)
            pe.transpose(psum[0:2 * E, 7, P:2 * P], oh2, ident[:]).then_inc(oh_turned, 1)
            pe.wait_ge(gt_copied, 2)
            pe.wait_ge(b2_loaded, 16 * (P // E))
            for t in range(T):
                j = t % 4
                if t >= 2:
                    pe.wait_ge(h2_made, t - 1)
                for c in range(NC):
                    mm = pe.matmul(psum[:, 2 * (t % 2) + c], gt[j * E:(j + 1) * E, t // 4], b2r[j * E:(j + 1) * E, c * BANK:(c + 1) * BANK],
                                   start=True, stop=True)
                mm.then_inc(b2_done, 1)
            pe.wait_ge(tokens_loaded, 16)
            pe.transpose(psum[:, 5, 0:NBLK], tokens, ident[0:NBLK, 0:NBLK]).then_inc(tokens_turned, 1)


def expert_phase(nc, dram, keep):
    S, D = dram["x"].shape[1], dram["x"].shape[2]
    E, F = dram["w1"].shape[1], dram["w2"].shape[2]
    KD, KF = D // P, F // P
    FC = BANK // 2
    C1, C2 = F // FC, D // BANK
    CH = C1 + C2
    HALF = KD // 2
    PER_RAW = 2 * CH // RAW
    NBLK = blocks_bound(S, E)
    GROUPS = E + S * TOP_K // (2 * P)
    COLS = 8

    with ExitStack() as ctx:
        def sb(name, shape, dt=F32):
            return ctx.enter_context(nc.sbuf_tensor(name, shape, dt))

        sems = []

        def sem(name):
            sems.append(nc.alloc_semaphore(name=name))
            return sems[-1]

        raw, hl = keep["raw"], keep["hl"]
        xt = sb("xt", [P, 2, 2, KD, P], F32R)
        ht = sb("ht", [P, 2, 2, KF, P], F32R)
        sel = sb("sel", [2 * E, P], F32R)
        xg = sb("xg", [P, 2, D])
        y_sb = sb("y_sb", [P, C2, BANK])
        gu = sb("gu", [P, 2, 2 * FC])
        g1, u1 = gu[:, :, 0:FC], gu[:, :, FC:2 * FC]
        sg = sb("sg", [P, 2, FC])
        idx_cur = sb("idx_cur", [P, 2], U32)
        psum = ctx.enter_context(nc.psum_tensor("expert_psum", [P, 8, BANK], F32))
        X_BANK, HT_BANK = 4, 6

        AB = range(2)
        raw_loaded = [sem(f"moe_raw_loaded{s}") for s in range(RAW)]
        half_hi = sem("half_hi")
        half_lo = [sem(f"half_lo{s}") for s in range(RAW)]
        x_loaded = [sem(f"moe_x_loaded{b}") for b in AB]
        idx_made = [sem(f"idx_made{b}") for b in AB]
        x_turned = [sem(f"moe_x_turned{b}") for b in AB]
        xt_hi = [sem(f"xt_hi{b}") for b in AB]
        xt_lo = [sem(f"xt_lo{b}") for b in AB]
        sel_made = sem("sel_made")
        h_done = [sem(f"h_done{b}") for b in AB]
        clamped = [sem(f"clamped{b}") for b in AB]
        u_raised = [sem(f"u_raised{b}") for b in AB]
        sig_made = [sem(f"sig_made{b}") for b in AB]
        gate_made = [sem(f"gate_made{b}") for b in AB]
        hid_made = [sem(f"hid_made{b}") for b in AB]
        hid_turned = [sem(f"hid_turned{b}") for b in AB]
        ht_hi = [sem(f"ht_hi{b}") for b in AB]
        ht_lo = [sem(f"ht_lo{b}") for b in AB]
        y_done = [[sem(f"y_done{b}{c}") for c in range(C2)] for b in AB]
        y_copied = [[sem(f"y_copied{b}{c}") for c in range(C2)] for b in AB]
        y_stored = [sem(f"y_stored{c}") for c in range(C2)]
        passed = {n: sem(f"moe_passed_{n}") for n in ("sp", "act", "dve", "pe", "pool")}

        w1e = dram["w1"][0].rearrange("e (k p) n -> e p k n", p=P)
        w2e = dram["w2"][0].rearrange("e (k p) n -> e p k n", p=P)
        wg3 = dram["w_ple_gate"][0].rearrange("(k p) n -> p k n", p=P)
        wp3 = dram["w_ple_proj"][0].rearrange("(k p) n -> p k n", p=P)
        y_blocks = dram["y_slots"].rearrange("(b p) d -> b p d", p=P)
        tab = keep["tab"]

        def entry(eng, g, col, top):
            return eng.value_load(tab[0:1, bass.ds(g * COLS + col, 1)], min_val=0, max_val=top)

        def seconds(eng, g):
            return entry(eng, g, 2, 1), entry(eng, g, 4, GROUPS)

        @contextmanager
        def each_group(eng):
            with eng.Fori(0, GROUPS // 8) as eight:
                some = entry(eng, eight * 8, 3, 1)
                with eng.If(some > 0):
                    with eng.Fori(0, 8) as i:
                        g = eight * 8 + i
                        valid = entry(eng, g, 3, 1)
                        with eng.If(valid > 0):
                            yield g

        block = ctx.enter_context(phase_block(nc, sems))

        @block.sync
        def _(sp):
            with each_group(sp) as g:
                e = entry(sp, g, 0, E - 1)
                for m in range(2 * CH):
                    c, z, r = m // 2, m % 2, m % RAW
                    if m < RAW:
                        with sp.If(g > 0):
                            sp.wait_ge(half_lo[r], g * PER_RAW)
                            sp.sem_inc(passed["sp"], 1)
                    else:
                        sp.wait_ge(half_lo[r], g * PER_RAW + m // RAW)
                    for y in range(2):
                        k2 = z * HALF + y * (HALF // 2)
                        if c < C1:
                            src = w1e[bass.ds(e, 1), :, z * HALF:(z + 1) * HALF, y * F + c * FC:y * F + (c + 1) * FC]
                            dst = raw[:, r, :, y * FC:(y + 1) * FC]
                        else:
                            src = w2e[bass.ds(e, 1), :, k2:k2 + HALF // 2, (c - C1) * BANK:(c - C1 + 1) * BANK]
                            dst = raw[:, r, y * (HALF // 2):(y + 1) * (HALF // 2)]
                        sp.dma_start(dst, src.rearrange("o p k n -> (o p) k n")).then_inc(raw_loaded[r], 16)
                more = entry(sp, g + 1, 3, 1)
                with sp.If(more < 1):
                    for m in range(5):
                        c, z = m // 2, m % 2
                        sp.wait_ge(half_lo[m], g * PER_RAW + PER_RAW)
                        for y in range(2):
                            if m < 4:
                                k2 = z * HALF + y * (HALF // 2)
                                src = wg3[:, k2:k2 + HALF // 2, c * BANK:(c + 1) * BANK]
                                dst = raw[:, m, y * (HALF // 2):(y + 1) * (HALF // 2)]
                            else:
                                src = wp3[:, y:y + 1]
                                dst = raw[:, m].rearrange("p k n -> p (k n)").rearrange("p (k n) -> p k n", k=2)[:, y:y + 1]
                            sp.dma_start(dst, src).then_inc(raw_loaded[m], 16)

        @block.gpsimd
        def _(pool):
            def gather(b, n, block_id):
                pool.tensor_copy(idx_cur[:, b:b + 1], keep["idx"][:, bass.ds(block_id, 1)]).then_inc(idx_made[b], 1)
                pool.wait_ge(idx_made[b], n + 1)
                pool.sem_inc(passed["pool"], 1)
                pool.indirect_dma_start(out=xg[:, b], out_offset=None, in_=dram["hn_rows"],
                                        in_offset=bass.IndirectOffsetOnAxis(ap=idx_cur[:, b:b + 1], axis=0)).then_inc(x_loaded[b], 16)

            def raise_up(b, n, c):
                pool.wait_ge(clamped[b], n * C1 + c + 1)
                pool.sem_inc(passed["pool"], 1)
                pool.tensor_scalar(u1[:, b], u1[:, b], -LIMIT, 1.0, ALU.max, ALU.add).then_inc(u_raised[b], 1)

            def hidden(b, n, c):
                pool.wait_ge(sig_made[b], n * C1 + c + 1)
                pool.wait_ge(clamped[b], n * C1 + c + 1)
                pool.tensor_tensor(sg[:, b], g1[:, b], sg[:, b], ALU.mult).then_inc(gate_made[b], 1)
                pool.wait_ge(gate_made[b], n * C1 + c + 1)
                pool.wait_ge(u_raised[b], n * C1 + c + 1)
                pool.tensor_tensor(u1[:, b], u1[:, b], sg[:, b], ALU.mult).then_inc(hid_made[b], 1)

            has2, _n = seconds(pool, 0)
            blk = entry(pool, 0, 1, NBLK - 2)
            gather(0, 0, blk)
            with pool.If(has2 > 0):
                gather(1, 0, blk + 1)
            with each_group(pool) as g:
                more = entry(pool, g + 1, 3, 1)
                with pool.If(more > 0):
                    has2, before = seconds(pool, g + 1)
                    blk = entry(pool, g + 1, 1, NBLK - 2)
                    pool.wait_ge(x_loaded[0], g * 16 + 16)
                    pool.wait_ge(x_turned[0], g * 2 + 2)
                    gather(0, g + 1, blk)
                    with pool.If(has2 > 0):
                        with pool.If(before > 0):
                            pool.wait_ge(x_loaded[1], before * 16)
                            pool.wait_ge(x_turned[1], before * 2)
                            pool.sem_inc(passed["pool"], 1)
                        gather(1, before, blk + 1)
                has2, n2 = seconds(pool, g)

                def both(step, *args):
                    with pool.If(has2 > 0):
                        step(1, n2, *args)
                    step(0, g, *args)

                for c in range(C1):
                    both(raise_up, c)
                    both(hidden, c)

        @block.scalar
        def _(act):
            def split_hi(g, c, z):
                if z == 0:
                    if c == 0:
                        act.wait_ge(h_done[0], g * C1)
                    elif c == 1:
                        act.wait_ge(y_done[0][0], g)
                    elif c == 2:
                        with act.If(g > 0):
                            act.wait_ge(y_done[0][1], g)
                            act.sem_inc(passed["act"], 1)
                    else:
                        act.wait_ge(h_done[0], g * C1 + (c - 2))
                m = 2 * c + z
                act.wait_ge(raw_loaded[m % RAW], (g * PER_RAW + m // RAW + 1) * 32)
                act.activation(hl[:, c % HL, 0, z * HALF:(z + 1) * HALF], raw[:, m % RAW], ACT.Copy).then_inc(half_hi, 1)

            def tokens_hi(b, n):
                for q in range(2):
                    act.wait_ge(x_turned[b], n * 2 + q + 1)
                    act.activation(xt[:, b, 0, 4 * q:4 * q + 4], psum[:, X_BANK + q].rearrange("p (k m) -> p k m", k=4),
                                   ACT.Copy).then_inc(xt_hi[b], 1)

            def sigmoid(b, n, c):
                if c == 0:
                    with act.If(n > 0):
                        act.wait_ge(hid_made[b], n * C1)
                        act.sem_inc(passed["act"], 1)
                else:
                    act.wait_ge(hid_made[b], n * C1 + c)
                act.wait_ge(clamped[b], n * C1 + c + 1)
                act.activation(sg[:, b], g1[:, b], ACT.Sigmoid, scale=ALPHA).then_inc(sig_made[b], 1)

            def hidden_hi(b, n, c):
                act.wait_ge(hid_turned[b], n * C1 + c + 1)
                act.activation(ht[:, b, 0, 2 * c:2 * c + 2], psum[:, HT_BANK + b, 0:FC].rearrange("p (k m) -> p k m", k=2),
                               ACT.Copy).then_inc(ht_hi[b], 1)

            def results(b, n, c, block_id, stores):
                with act.If(stores > 0):
                    act.wait_ge(y_stored[c], stores * 16)
                    act.sem_inc(passed["act"], 1)
                act.wait_ge(y_done[b][c], n + 1)
                act.activation(y_sb[:, c], psum[:, 2 * b + c % 2], ACT.Copy).then_inc(y_copied[b][c], 1)
                act.wait_ge(y_copied[b][c], n + 1)
                dst = y_blocks[bass.ds(block_id, 1), :, c * BANK:(c + 1) * BANK].rearrange("o p n -> (o p) n")
                act.dma_start(dst, y_sb[:, c]).then_inc(y_stored[c], 16)

            has2, before = seconds(act, 0)
            tokens_hi(0, 0)
            with act.If(has2 > 0):
                tokens_hi(1, 0)
            for m in range(4):
                act.wait_ge(raw_loaded[m], 32)
                act.activation(hl[:, m // 2, 0, m % 2 * HALF:(m % 2 + 1) * HALF], raw[:, m], ACT.Copy).then_inc(half_hi, 1)
            with each_group(act) as g:
                split_hi(g, 2, 0)
                split_hi(g, 2, 1)
                has2, n2 = seconds(act, g)

                def both(step, *args):
                    with act.If(has2 > 0):
                        step(1, n2, *args)
                    step(0, g, *args)

                for c in range(C1):
                    if c >= 1:
                        split_hi(g, c + 2, 0)
                        split_hi(g, c + 2, 1)
                        both(hidden_hi, c - 1)
                    both(sigmoid, c)
                more = entry(act, g + 1, 3, 1)
                both(hidden_hi, C1 - 1)
                with act.If(more > 0):
                    tokens_hi(0, g + 1)
                for z in range(2):
                    split_hi(g + 1, 0, z)
                more2, n2_more = seconds(act, g + 1)
                with act.If(more2 > 0):
                    tokens_hi(1, n2_more)
                blk = entry(act, g, 1, NBLK - 2)
                with act.If(has2 > 0):
                    results(1, n2, 0, blk + 1, n2 + g)
                results(0, g, 0, blk, n2 + has2 + g)
                for z in range(2):
                    split_hi(g + 1, 1, z)
                with act.If(has2 > 0):
                    results(1, n2, 1, blk + 1, n2 + g)
                results(0, g, 1, blk, n2 + has2 + g)
                with act.If(more < 1):
                    split_hi(g + 1, 2, 0)
            groups, with2 = entry(act, 0, 6, GROUPS), entry(act, 0, 5, GROUPS)
            for c in range(C2):
                act.wait_ge(y_stored[c], (groups + with2) * 16)
            act.sem_inc(passed["act"], 1)

        @block.vector
        def _(dve):
            def split_lo(g, c, z):
                m, ks = 2 * c + z, slice(z * HALF, (z + 1) * HALF)
                dve.wait_ge(half_hi, g * (2 * CH) + (m + 1))
                dve.tensor_tensor(hl[:, c % HL, 1, ks], raw[:, m % RAW], hl[:, c % HL, 0, ks].bitcast(F32),
                                  ALU.subtract).then_inc(half_lo[m % RAW], 1)

            def tokens_lo(b, n):
                for q in range(2):
                    dve.wait_ge(xt_hi[b], n * 2 + q + 1)
                    dve.tensor_tensor(xt[:, b, 1, 4 * q:4 * q + 4], psum[:, X_BANK + q].rearrange("p (k m) -> p k m", k=4),
                                      xt[:, b, 0, 4 * q:4 * q + 4].bitcast(F32), ALU.subtract).then_inc(xt_lo[b], 1)

            def clamp(b, n, c):
                if c == 0:
                    with dve.If(n > 0):
                        dve.wait_ge(hid_turned[b], n * C1)
                        dve.sem_inc(passed["dve"], 1)
                else:
                    dve.wait_ge(hid_turned[b], n * C1 + c)
                dve.wait_ge(h_done[b], n * C1 + c + 1)
                dve.tensor_scalar(gu[:, b], psum[:, 2 * b + c % 2], LIMIT, None, ALU.min).then_inc(clamped[b], 1)

            def hidden_lo(b, n, c):
                dve.wait_ge(ht_hi[b], n * C1 + c + 1)
                dve.tensor_tensor(ht[:, b, 1, 2 * c:2 * c + 2], psum[:, HT_BANK + b, 0:FC].rearrange("p (k m) -> p k m", k=2),
                                  ht[:, b, 0, 2 * c:2 * c + 2].bitcast(F32), ALU.subtract).then_inc(ht_lo[b], 1)

            def pick(g):
                dve.tensor_copy(sel[:], keep["sel_all"][:, bass.ds(g, 1)].broadcast_to([2 * E, P])).then_inc(sel_made, 1)

            has2, _n = seconds(dve, 0)
            dve.tensor_copy(sel[:], keep["sel_all"][:, 0:1].broadcast_to([2 * E, P])).then_inc(sel_made, 1)
            tokens_lo(0, 0)
            with dve.If(has2 > 0):
                tokens_lo(1, 0)
            for m in range(4):
                split_lo(0, m // 2, m % 2)
            with each_group(dve) as g:
                split_lo(g, 2, 0)
                has2, n2 = seconds(dve, g)

                def both(step, *args):
                    with dve.If(has2 > 0):
                        step(1, n2, *args)
                    step(0, g, *args)

                for c in range(C1):
                    if c >= 1:
                        split_lo(g, c + 2, 0)
                    both(clamp, c)
                    if c >= 1:
                        both(hidden_lo, c - 1)
                    split_lo(g, c + 2, 1)
                both(hidden_lo, C1 - 1)
                more = entry(dve, g + 1, 3, 1)
                more2, n2_more = seconds(dve, g + 1)
                with dve.If(more > 0):
                    pick(g + 1)
                    tokens_lo(0, g + 1)
                for z in range(2):
                    split_lo(g + 1, 0, z)
                with dve.If(more2 > 0):
                    tokens_lo(1, n2_more)
                for z in range(2):
                    split_lo(g + 1, 1, z)
                with dve.If(more < 1):
                    split_lo(g + 1, 2, 0)

        @block.tensor
        def _(pe):
            ident = keep["ident"]

            def turn_tokens(b, n):
                pe.wait_ge(x_loaded[b], n * 16 + 16)
                for q in range(2):
                    for k in range(4):
                        mm = pe.transpose(psum[:, X_BANK + q, k * P:(k + 1) * P], xg[:, b, (4 * q + k) * P:(4 * q + k + 1) * P], ident[:])
                    mm.then_inc(x_turned[b], 1)

            def turn_hidden(b, n, c):
                if c > 0:
                    pe.wait_ge(ht_lo[b], n * C1 + c)
                pe.wait_ge(hid_made[b], n * C1 + c + 1)
                for k in range(2):
                    mm = pe.transpose(psum[:, HT_BANK + b, k * P:(k + 1) * P], u1[:, b, k * P:(k + 1) * P], ident[:])
                mm.then_inc(hid_turned[b], 1)

            def half_ready(g, c, z):
                m = 2 * c + z
                pe.wait_ge(half_lo[m % RAW], g * PER_RAW + (m // RAW + 1))

            def up_half(b, n, g, c, z):
                bank = psum[:, 2 * b + c % 2]
                if z == 0:
                    if c < 2:
                        with pe.If(n > 0):
                            pe.wait_ge(y_copied[b][c], n)
                            pe.sem_inc(passed["pe"], 1)
                        if c == 0:
                            pe.wait_ge(xt_lo[b], n * 2 + 2)
                    else:
                        pe.wait_ge(clamped[b], n * C1 + (c - 1))
                    bias = keep["b1s"][:].rearrange("e (z f) -> e z f", z=2)[:, :, c * FC:(c + 1) * FC]
                    pe.matmul(bank.rearrange("p (z f) -> p z f", z=2), sel[:], bias, start=True, stop=False)
                else:
                    half_ready(g, c, 1)
                s = c % HL
                for k in range(z * HALF, (z + 1) * HALF):
                    mm = split_mm(pe, bank, xt[:, b, 0, k], xt[:, b, 1, k], hl[:, s, 0, k], hl[:, s, 1, k], False, k == KD - 1)
                if z == 1:
                    mm.then_inc(h_done[b], 1)

            def down_part(b, n, g, c, ks):
                bank = psum[:, 2 * b + c % 2]
                if ks[0] == 0:
                    pe.wait_ge(clamped[b], n * C1 + (c - 1))
                if c == C1:
                    pe.wait_ge(ht_lo[b], n * C1 + ks[-1] // 2 + 1)
                s = c % HL
                for k in ks:
                    if k == HALF:
                        half_ready(g, c, 1)
                    mm = split_mm(pe, bank, ht[:, b, 0, k], ht[:, b, 1, k], hl[:, s, 0, k], hl[:, s, 1, k], k == 0, k == KF - 1)
                if ks[-1] == KF - 1:
                    mm.then_inc(y_done[b][c - C1], 1)
                return mm

            has2, _n = seconds(pe, 0)
            turn_tokens(0, 0)
            with pe.If(has2 > 0):
                pe.wait_ge(xt_lo[0], 2)
                turn_tokens(1, 0)
            with each_group(pe) as g:
                has2, n2 = seconds(pe, g)

                def both(step, *args):
                    with pe.If(has2 > 0):
                        step(1, n2, *args)
                    return step(0, g, *args)

                pe.wait_ge(sel_made, g + 1)
                for c in range(C1):
                    half_ready(g, c, 0)
                    pe.sem_inc(passed["pe"], 1)
                    with pe.If(has2 > 0):
                        up_half(1, n2, g, c, 0)
                        up_half(1, n2, g, c, 1)
                    up_half(0, g, g, c, 0)
                    up_half(0, g, g, c, 1)
                    if c >= 1:
                        both(turn_hidden, c - 1)
                c = C1
                half_ready(g, c, 0)
                pe.sem_inc(passed["pe"], 1)
                both(down_part, g, c, range(0, 4))
                more = entry(pe, g + 1, 3, 1)
                more2, n2_more = seconds(pe, g + 1)
                with pe.If(more > 0):
                    turn_tokens(0, g + 1)
                both(turn_hidden, C1 - 1)
                both(down_part, g, c, range(4, 6))
                both(down_part, g, c, range(6, 8))
                with pe.If(more2 > 0):
                    pe.wait_ge(xt_lo[0], (g + 2) * 2)
                    turn_tokens(1, n2_more)
                c = C1 + 1
                half_ready(g, c, 0)
                pe.sem_inc(passed["pe"], 1)
                both(down_part, g, c, range(0, 8))


def embed_phase(nc, dram, keep):
    S, D = dram["x"].shape[1], dram["x"].shape[2]
    T, KD, NC = S // P, D // P, D // BANK
    PLE = dram["p"].shape[3]
    KP = PLE // P
    with ExitStack() as ctx:
        def sb(name, shape, dt=F32):
            return ctx.enter_context(nc.sbuf_tensor(name, shape, dt))

        sems = []

        def sem(name):
            sems.append(nc.alloc_semaphore(name=name))
            return sems[-1]

        wg = keep["hl"]
        wp = keep["hl"][:, 2, :, 0:HALF_K].rearrange("p z k n -> p z (k n)").rearrange("p z (k n) -> p z k n", k=KP)
        ar = keep["raw"][:].rearrange("p r k n -> p (r k n)")
        yg = ar[:, 0:4 * D].rearrange("p (k d) -> p k d", k=TOP_K)
        h_in = ar[:, 4 * D:6 * D].rearrange("p (b d) -> p b d", b=2)
        g_ple, g_post, g_fin = (ar[:, i * D:(i + 1) * D] for i in (6, 7, 8))
        hn, sg, junk = (ar[:, i * D:(i + 1) * D] for i in (9, 10, 11))
        h = sb("h4", [P, 2, D])
        hnt = sb("hnt4", [P, 2, 2, KD, P], F32R)
        p_sb = sb("p_sb", [P, 2, PLE])
        pt = sb("p_t", [P, 2, KP, P], F32R)
        ple = sb("ple", [P, D])
        ss = sb("ss4", [P, 3, 3])
        OUT, EMB, HID = 0, 1, 2
        psum = ctx.enter_context(nc.psum_tensor("embed_psum", [P, 8, BANK], F32))
        gate_ps = [psum[:, 4 * b:4 * b + 2].rearrange("p b n -> p (b n)") for b in range(2)]
        HN_BANK, P_BANK = 2, 2
        ple_ps = psum[:, 6:8].rearrange("p b n -> p (b n)")

        par_loaded = sem("embed_par_loaded")
        p_loaded = [sem(f"p_loaded{b}") for b in range(2)]
        h_loaded = [sem(f"h_loaded{b}") for b in range(2)]
        y_loaded = [sem(f"y_loaded{k}") for k in range(TOP_K)]
        p_turned = sem("p_turned")
        pt_hi = sem("p_hi")
        pt_lo = sem("p_lo")
        ple_done = sem("ple_done")
        ple_made = sem("ple_made")
        combined = sem("combined")
        h_squared = sem("h_squared4")
        ple_squared = sem("ple_squared")
        out_squared = sem("out_squared")
        roots = sem("roots4")
        inverses = sem("inverses4")
        hn_made = sem("hn_made4")
        hn_turned = sem("hn_turned4")
        hnt_hi = sem("hnt_hi")
        hnt_lo = sem("hnt_lo")
        gate_done = sem("gate_done")
        sig_made = sem("sig_made4")
        gated = sem("gated")
        h_final = sem("h_final")
        out_made = sem("out_made")
        out_stored = sem("out_stored")
        act_passed = sem("act_passed4")
        pe_passed = sem("pe_passed4")

        h_rows = dram["h_rows"].rearrange("(t p) d -> p t d", p=P)
        out_rows = dram["out"][0].rearrange("(t p) d -> p t d", p=P)
        p_rows = dram["p"][0, 0].rearrange("(t p) c -> p t c", p=P)

        block = ctx.enter_context(phase_block(nc, sems))


        @block.sync
        def _(sp):
            for b in range(2):
                sp.dma_start(h_in[:, b:b + 1], h_rows[:, b:b + 1]).then_inc(h_loaded[b], 16)
                sp.dma_start(p_sb[:, b:b + 1], p_rows[:, b:b + 1]).then_inc(p_loaded[b], 16)
            for g, name in ((g_ple, "ple_norm"), (g_post, "ple_post_norm")):
                sp.dma_start(g, dram[name][0:1, :].partition_broadcast(P)).then_inc(par_loaded, 16)
            sp.dma_start(g_fin, dram["final_norm"].rearrange("(o d) -> o d", o=1).partition_broadcast(P)).then_inc(par_loaded, 16)
            out_sb = sg.rearrange("p (o d) -> p o d", o=1)
            with sp.Fori(0, T // 2 - 1) as pair:
                for b in range(2):
                    t = pair * 2 + b
                    sp.wait_ge(combined, t * TOP_K + 1)
                    sp.dma_start(h_in[:, b:b + 1], h_rows[:, bass.ds(t + 2, 1)]).then_inc(h_loaded[b], 16)
                    sp.wait_ge(p_turned, t + 1)
                    sp.dma_start(p_sb[:, b:b + 1], p_rows[:, bass.ds(t + 2, 1)]).then_inc(p_loaded[b], 16)
                    sp.wait_ge(out_made, t + 1)
                    sp.dma_start(out_rows[:, bass.ds(t, 1)], out_sb).then_inc(out_stored, 16)
            for t in (T - 2, T - 1):
                sp.wait_ge(out_made, t + 1)
                sp.dma_start(out_rows[:, t:t + 1], out_sb).then_inc(out_stored, 16)
            sp.wait_ge(out_stored, 16 * T)

        @block.gpsimd
        def _(pool):
            for t in range(T):
                for k in range(TOP_K):
                    if t >= 1:
                        pool.wait_ge(combined, (t - 1) * TOP_K + k + 1)
                    pool.indirect_dma_start(out=yg[:, k], out_offset=None, in_=dram["y_slots"],
                                            in_offset=bass.IndirectOffsetOnAxis(ap=keep["slots"][:, t, k:k + 1], axis=0)).then_inc(y_loaded[k], 16)

        @block.scalar
        def _(act):
            def embedding_hi(t):
                act.wait_ge(p_turned, t + 1)
                act.wait_ge(ple_done, t)
                act.activation(pt[:, 0], psum[:, P_BANK, 0:PLE].rearrange("p (k m) -> p k m", k=KP), ACT.Copy).then_inc(pt_hi, 1)

            def turned_hi(t, b):
                for q in range(2):
                    act.wait_ge(hn_turned, t * 2 + (q + 1))
                    act.activation(hnt[:, b, 0, 4 * q:4 * q + 4], psum[:, HN_BANK + q].rearrange("p (k m) -> p k m", k=4),
                                   ACT.Copy).then_inc(hnt_hi, 1)

            def sigmoid(t, b):
                act.wait_ge(gate_done, t + 1)
                act.activation(sg, gate_ps[b], ACT.Sigmoid).then_inc(sig_made, 1)

            def square_embedding(t):
                act.wait_ge(ple_done, t + 1)
                act.activation(junk, ple_ps, ACT.Square, accum_out=ss[:, 0, EMB:EMB + 1]).then_inc(ple_squared, 1)
                act.wait_ge(ple_squared, t + 1)

            def square_output(t):
                act.wait_ge(h_final, t + 1)
                act.activation(junk, sg, ACT.Square, accum_out=ss[:, 0, OUT:OUT + 1]).then_inc(out_squared, 1)
                act.wait_ge(out_squared, t + 1)

            def square_h(t, b):
                act.wait_ge(combined, t * TOP_K + TOP_K)
                act.activation(junk, h[:, b], ACT.Square, accum_out=ss[:, 0, HID:HID + 1]).then_inc(h_squared, 1)
                act.wait_ge(h_squared, t + 1)

            def root(a, z):
                act.activation(ss[:, 1, a:z + 1], ss[:, 0, a:z + 1], ACT.Sqrt, scale=1.0 / D, bias=keep["eps"][:, 0:1]).then_inc(roots, 1)

            square_h(0, 0)
            root(HID, HID)
            act.wait_ge(p_turned, 1)
            act.activation(pt[:, 0], psum[:, P_BANK, 0:PLE].rearrange("p (k m) -> p k m", k=KP), ACT.Copy).then_inc(pt_hi, 1)
            turned_hi(0, 0)
            square_embedding(0)
            square_h(1, 1)
            root(EMB, HID)
            embedding_hi(1)

            def turn(t, b, last=False):
                turned_hi(t + 1, 1 - b)
                if b == 0 and not isinstance(t, int):
                    with act.If(t > 0):
                        act.wait_ge(out_stored, t * 16)
                        act.sem_inc(act_passed, 1)
                else:
                    act.wait_ge(out_stored, t * 16)
                sigmoid(t, b)
                if not last:
                    embedding_hi(t + 2)
                square_embedding(t + 1)
                square_output(t)
                if not last:
                    square_h(t + 2, b)
                root(OUT, EMB if last else HID)

            with act.Fori(0, T // 2 - 1) as pair:
                for b in range(2):
                    turn(pair * 2 + b, b)
            turn(T - 2, 0, last=True)
            act.wait_ge(out_stored, (T - 1) * 16)
            sigmoid(T - 1, 1)
            square_output(T - 1)
            root(OUT, OUT)

        @block.vector
        def _(dve):
            def embedding_lo(t):
                dve.wait_ge(pt_hi, t + 1)
                dve.tensor_tensor(pt[:, 1], psum[:, P_BANK, 0:PLE].rearrange("p (k m) -> p k m", k=KP),
                                  pt[:, 0].bitcast(F32), ALU.subtract).then_inc(pt_lo, 1)

            def turned_lo(t, b):
                for q in range(2):
                    dve.wait_ge(hnt_hi, t * 2 + (q + 1))
                    dve.tensor_tensor(hnt[:, b, 1, 4 * q:4 * q + 4], psum[:, HN_BANK + q].rearrange("p (k m) -> p k m", k=4),
                                      hnt[:, b, 0, 4 * q:4 * q + 4].bitcast(F32), ALU.subtract).then_inc(hnt_lo, 1)

            def combine(t, b, loads):
                dve.wait_ge(h_loaded[b], loads * 16)
                for k in range(TOP_K):
                    dve.wait_ge(y_loaded[k], t * 16 + 16)
                    gate = keep["gates"][:, t:t + 1, k] if isinstance(t, int) else keep["gates"][:, bass.ds(t, 1), k]
                    dve.scalar_tensor_tensor(out=h[:, b], in0=yg[:, k], scalar=gate, in1=h_in[:, b] if k == 0 else h[:, b],
                                             op0=ALU.mult, op1=ALU.add).then_inc(combined, 1)
                    dve.wait_ge(combined, t * TOP_K + (k + 1))

            def invert(n, a, z):
                dve.wait_ge(roots, n)
                dve.reciprocal(ss[:, 2, a:z + 1], ss[:, 1, a:z + 1]).then_inc(inverses, 1)
                dve.wait_ge(inverses, n)

            def norm_h(t, b):
                dve.wait_ge(hn_turned, t * 2)
                dve.scalar_tensor_tensor(out=hn, in0=h[:, b], scalar=ss[:, 2, HID:HID + 1], in1=g_ple,
                                         op0=ALU.mult, op1=ALU.mult).then_inc(hn_made, 1)

            def norm_embedding():
                dve.scalar_tensor_tensor(out=ple[:], in0=ple_ps, scalar=ss[:, 2, EMB:EMB + 1], in1=g_post,
                                         op0=ALU.mult, op1=ALU.mult).then_inc(ple_made, 1)

            def gate_and_add(t, b):
                dve.wait_ge(sig_made, t + 1)
                dve.wait_ge(ple_made, t + 1)
                dve.tensor_tensor(sg, sg, ple[:], ALU.mult).then_inc(gated, 1)
                dve.wait_ge(gated, t + 1)
                dve.tensor_tensor(sg, h[:, b], sg, ALU.add).then_inc(h_final, 1)
                dve.wait_ge(h_final, t + 1)

            def norm_output():
                dve.scalar_tensor_tensor(out=sg, in0=sg, scalar=ss[:, 2, OUT:OUT + 1], in1=g_fin,
                                         op0=ALU.mult, op1=ALU.mult).then_inc(out_made, 1)

            combine(0, 0, 1)
            invert(1, HID, HID)
            dve.wait_ge(par_loaded, 48)
            dve.scalar_tensor_tensor(out=hn, in0=h[:, 0], scalar=ss[:, 2, HID:HID + 1], in1=g_ple,
                                     op0=ALU.mult, op1=ALU.mult).then_inc(hn_made, 1)
            embedding_lo(0)
            turned_lo(0, 0)
            combine(1, 1, 1)
            invert(2, EMB, HID)
            norm_h(1, 1)
            norm_embedding()
            embedding_lo(1)

            def turn(t, b, loads=0, last=False):
                turned_lo(t + 1, 1 - b)
                gate_and_add(t, b)
                if not last:
                    embedding_lo(t + 2)
                if not last:
                    combine(t + 2, b, loads)
                invert(t + 3, OUT, EMB if last else HID)
                if not last:
                    norm_h(t + 2, b)
                norm_output()
                norm_embedding()

            with dve.Fori(0, T // 2 - 1) as pair:
                for b in range(2):
                    turn(pair * 2 + b, b, pair + 2)
            turn(T - 2, 0, last=True)
            gate_and_add(T - 1, 1)
            invert(T + 2, OUT, OUT)
            norm_output()

        @block.tensor
        def _(pe):
            ident = keep["ident"]

            def turn_embedding(t, b, loads):
                pe.wait_ge(p_loaded[b], loads * 16)
                for k in range(KP):
                    mm = pe.transpose(psum[:, P_BANK, k * P:(k + 1) * P], p_sb[:, b, k * P:(k + 1) * P], ident[:])
                mm.then_inc(p_turned, 1)

            def project_embedding(t):
                pe.wait_ge(pt_lo, t + 1)
                for c in range(NC):
                    for k in range(KP):
                        mm = split_mm(pe, psum[:, 6 + c], pt[:, 0, k], pt[:, 1, k], wp[:, 0, k, c * BANK:(c + 1) * BANK],
                                      wp[:, 1, k, c * BANK:(c + 1) * BANK], k == 0, k == KP - 1)
                mm.then_inc(ple_done, 1)

            def turn_h(t):
                pe.wait_ge(pt_lo, t + 1)
                pe.wait_ge(hn_made, t + 1)
                for q in range(2):
                    for k in range(4):
                        mm = pe.transpose(psum[:, HN_BANK + q, k * P:(k + 1) * P], hn[:, (4 * q + k) * P:(4 * q + k + 1) * P], ident[:])
                    mm.then_inc(hn_turned, 1)

            def gate_product(t, b):
                for c in range(NC):
                    for k in range(KD):
                        mm = split_mm(pe, psum[:, 4 * b + c], hnt[:, b, 0, k], hnt[:, b, 1, k], wg[:, c, 0, k], wg[:, c, 1, k],
                                      k == 0, k == KD - 1)
                mm.then_inc(gate_done, 1)

            def turn(t, b, loads):
                pe.wait_ge(hnt_lo, t * 2 + 2)
                turn_embedding(t + 1, 1 - b, loads)
                gate_product(t, b)
                turn_h(t + 1)
                pe.wait_ge(ple_made, t + 1)
                project_embedding(t + 1)

            turn_embedding(0, 0, 1)
            turn_h(0)
            project_embedding(0)
            with pe.Fori(0, T // 2 - 1) as pair:
                for b in range(2):
                    t = pair * 2 + b
                    turn(t, b, pair + b + 1)
                    if b == 1:
                        pe.wait_ge(sig_made, t)
                        pe.sem_inc(pe_passed, 1)
                    else:
                        with pe.If(pair > 0):
                            pe.wait_ge(sig_made, t)
                            pe.sem_inc(pe_passed, 1)
            turn(T - 2, 0, T // 2)
            pe.wait_ge(hnt_lo, 2 * T)
            pe.wait_ge(sig_made, T - 2)
            gate_product(T - 1, 1)


INPUTS = ["x", "p", "positions", "mix_norm", "w_in", "q_norm", "w_uq", "kv_norm", "w_ukv", "conv_w",
          "attn_out_norm", "conv_out_norm", "w_o", "moe_norm", "w_router", "b_router", "w1", "b1", "w2", "b2",
          "ple_norm", "w_ple_gate", "w_ple_proj", "ple_post_norm", "final_norm"]


def angle_constants():
    import numpy as np
    half = ROPE // 2
    freq = (np.float32(ROPE_THETA) ** (-np.arange(half, dtype=np.float32) / np.float32(half))).astype(np.float32)
    c = np.zeros((P, 4), np.float32)
    c[:, 0] = np.tile(freq, P // half)
    c[:ROPE, 1] = 0.25
    c[:ROPE, 2] = math.pi / 2
    c[:, 3] = 1.0
    c[ROPE:ROPE + half, 3] = -1.0
    return c


def build(nc, dram):
    S, D, E = dram["x"].shape[1], dram["x"].shape[2], dram["w1"].shape[1]
    for name, shape, dt in (("hn_rows", (S, D), F32), ("h_rows", (S, D), F32), ("row_tok", (blocks_bound(S, E) * P, 1), F32),
                            ("y_slots", (blocks_bound(S, E) * P, D), F32), ("table", (P, 8), I32)):
        dram[name] = nc.dram_tensor(name, shape, dt, kind="Internal").ap()
    with ExitStack() as ctx:
        def sb(name, shape, dt=F32):
            return ctx.enter_context(nc.sbuf_tensor(name, shape, dt))

        keep = {"ident": sb("ident", [P, P]), "ones": sb("ones", [P, P]), "eps": sb("eps", [P, 1])}
        with ExitStack() as mixed:
            for name, shape, dt in (("ss_att", [P, S // P, N_HEADS], F32), ("ss_conv", [P, S // P], F32),
                                    ("wide", [P, 2, 8 * S], F32R), ("conv", [P, 2, dram["conv_w"].shape[2] // P, S], F32R)):
                keep[name] = mixed.enter_context(nc.sbuf_tensor(name, shape, dt, side="right"))
            mix_phase(nc, dram, keep)
            keep.update({
                "gates": sb("gates", [P, S // P, TOP_K]), "slots": sb("slots", [P, S // P, TOP_K], U32),
                "tab": sb("tab", [1, P // 2 * 8], I32), "idx": sb("idx", [P, blocks_bound(S, E)], U32),
                "sel_all": sb("sel_all", [2 * E, P]), "b1s": sb("b1s", [2 * E, dram["b1"].shape[2]], F32R),
            })
            route_phase(nc, dram, keep)
        keep.update({"raw": sb("raw", [P, RAW, HALF_K, BANK]), "hl": sb("hl", [P, HL, 2, 2 * HALF_K, BANK], F32R)})
        expert_phase(nc, dram, keep)
        embed_phase(nc, dram, keep)


def kernel(**inputs):
    import numpy as np
    import concourse.bacc as bacc
    from concourse.bass_utils import run_bass_kernel_spmd as run

    nc = bacc.Bacc("TRN2", target_bir_lowering=False, num_devices=1)
    arrays, dram = {}, {}
    for name in INPUTS:
        a = np.ascontiguousarray(inputs[name])
        arrays[f"in_{name}"] = a
        dram[name] = nc.dram_tensor(f"in_{name}", a.shape, mybir.dt.from_np(a.dtype), kind="ExternalInput").ap()
    arrays["angle_consts"] = angle_constants()
    dram["angle_consts"] = nc.dram_tensor("angle_consts", (P, 4), F32, kind="ExternalInput").ap()
    shape = tuple(inputs["x"].shape)
    dram["out"] = nc.dram_tensor("out_0", shape, F32, kind="ExternalOutput").ap()
    build(nc, dram)
    r = run(nc, [arrays], core_ids=[0])
    return r.results[0]["out_0"]
```
